# Optimizing a Trainium2 kernel written in Bass

```python
import math
import jax, jax.numpy as jnp
from jax import lax
import numpy as np

D_MODEL = 1024
BATCH = 1
SEQ = 512
DEPTH = 1

CHUNK = 64
EPS = 1e-6
MIX_WIDTH = D_MODEL
POOL_WIDTH = MIX_WIDTH // 2
POOL_WINDOWS = (2, 4, 8, 16)
N_POOL_GROUPS = len(POOL_WINDOWS)
POOL_GROUP = POOL_WIDTH // N_POOL_GROUPS
ATTN_WIDTH = MIX_WIDTH - POOL_WIDTH
HEAD_DIM = 64
N_HEADS = ATTN_WIDTH // HEAD_DIM
IDX_HEADS = 8
IDX_DIM = 64
TOPK_MAX = 256
Q_BLOCK = 128
PEER_HEADS = 8
PEER_KEYS = 128
PEER_EXPERTS = PEER_KEYS * PEER_KEYS
PEER_QDIM = 256
PEER_TOPK = 16
PEER_BLOCK = 128
NEG = -1e30

IN_SIZES = (POOL_WIDTH, ATTN_WIDTH, ATTN_WIDTH, ATTN_WIDTH, IDX_HEADS * IDX_DIM, IDX_DIM, IDX_HEADS)
IN_WIDTH = sum(IN_SIZES)
IN_SPLITS = tuple(int(s) for s in np.cumsum(IN_SIZES)[:-1])

kernel_name = "hymba_pool_dsa_peer_block"

def rms_norm(x, g):
    xf = x.astype(jnp.float32)
    y = xf * lax.rsqrt(jnp.mean(xf * xf, axis=-1, keepdims=True) + EPS)
    return (y * g.astype(jnp.float32)).astype(x.dtype)

def alibi_slopes(n_heads):
    h = jnp.arange(1, n_heads + 1, dtype=jnp.float32)
    return jnp.exp2(-8.0 * h / n_heads)

def pool_mixer(u, pool_w, pool_scale, pool_out_g):
    B, S, _ = u.shape
    uf = u.astype(jnp.float32)
    cs = jnp.cumsum(uf, axis=1)
    t = jnp.arange(S)
    parts = []
    for gi, win in enumerate(POOL_WINDOWS):
        lo, hi = gi * POOL_GROUP, (gi + 1) * POOL_GROUP
        cg = cs[..., lo:hi]
        prev = jnp.pad(cg, ((0, 0), (win, 0), (0, 0)))[:, :S]
        cnt = jnp.minimum(t + 1, win).astype(jnp.float32)[None, :, None]
        parts.append((cg - prev) / cnt - uf[..., lo:hi])
    pooled = jnp.stack(parts, axis=2).astype(u.dtype)
    mixed = jnp.einsum('bsgc,gcd->bsgd', pooled, pool_w).reshape(B, S, POOL_WIDTH)
    return rms_norm(mixed * pool_scale, pool_out_g)

def sparse_attention(q, k, v, qi, ki, wi, slopes):
    B, S = q.shape[0], q.shape[1]
    topk = min(TOPK_MAX, S // 4)
    s_chunk = jnp.arange(S) // CHUNK
    scale = HEAD_DIM ** -0.5

    def block(j):
        start = j * Q_BLOCK
        qb = lax.dynamic_slice_in_dim(q, start, Q_BLOCK, axis=1)
        qib = lax.dynamic_slice_in_dim(qi, start, Q_BLOCK, axis=1)
        wib = lax.dynamic_slice_in_dim(wi, start, Q_BLOCK, axis=1)
        t = start + jnp.arange(Q_BLOCK)
        t_chunk = t // CHUNK
        dots = jnp.einsum('bqhd,bsd->bqhs', qib, ki).astype(jnp.float32) * (IDX_DIM ** -0.5)
        score = jnp.einsum('bqh,bqhs->bqs', wib.astype(jnp.float32), jax.nn.relu(dots))
        admissible = s_chunk[None, :] <= t_chunk[:, None]
        score = jnp.where(admissible[None], score, NEG)
        _, sel = lax.top_k(score, topk)
        valid = (sel // CHUNK) <= t_chunk[None, :, None]
        kg = jax.vmap(lambda kb, ib: kb[ib])(k, sel)
        vg = jax.vmap(lambda vb, ib: vb[ib])(v, sel)
        logits = jnp.einsum('bqhd,bqkhd->bqhk', qb, kg).astype(jnp.float32) * scale
        dist = jnp.abs(t[None, :, None] - sel).astype(jnp.float32)
        logits = logits - slopes[None, None, :, None] * dist[:, :, None, :]
        logits = jnp.where(valid[:, :, None, :], logits, NEG)
        p = jax.nn.softmax(logits, axis=-1).astype(v.dtype)
        return jnp.einsum('bqhk,bqkhd->bqhd', p, vg)

    outs = lax.map(block, jnp.arange(S // Q_BLOCK))
    return jnp.swapaxes(outs, 0, 1).reshape(B, S, N_HEADS, HEAD_DIM)

def peer_ffn(h, wq, sub_keys, u_tab, v_tab):
    B, S, D = h.shape
    hb = h.reshape((B * S) // PEER_BLOCK, PEER_BLOCK, D)
    half = PEER_QDIM // 2

    def block(xb):
        q = (xb @ wq).reshape(PEER_BLOCK, PEER_HEADS, 2, half)
        s = jnp.einsum('thpd,hpnd->thpn', q, sub_keys).astype(jnp.float32)
        s1, i1 = lax.top_k(s[:, :, 0], PEER_TOPK)
        s2, i2 = lax.top_k(s[:, :, 1], PEER_TOPK)
        cand = (s1[..., :, None] + s2[..., None, :]).reshape(PEER_BLOCK, PEER_HEADS, PEER_TOPK * PEER_TOPK)
        cand_id = (i1[..., :, None] * PEER_KEYS + i2[..., None, :]).reshape(PEER_BLOCK, PEER_HEADS, PEER_TOPK * PEER_TOPK)
        top_s, pos = lax.top_k(cand, PEER_TOPK)
        eid = jnp.take_along_axis(cand_id, pos, axis=-1)
        g = jax.nn.softmax(top_s, axis=-1)
        ug = u_tab[eid]
        a = jax.nn.gelu(jnp.einsum('td,thkd->thk', xb, ug).astype(jnp.float32), approximate=False)
        vg = v_tab[eid]
        return jnp.einsum('thk,thkd->td', (g * a).astype(xb.dtype), vg)

    return lax.map(block, hb).reshape(B, S, D)

def setup_inputs(seed: int = 0) -> dict:
    key = jax.random.key(seed)
    ks = jax.random.split(key, 18)
    f32 = jnp.float32
    L = DEPTH
    D = D_MODEL

    def nrm(k, shape, std):
        return std * jax.random.normal(k, shape, f32)

    def gain(k, shape):
        return 1.0 + 0.1 * jax.random.normal(k, shape, f32)

    return {
        "x": jax.random.normal(ks[0], (BATCH, SEQ, D), f32),
        "c": jax.random.normal(ks[1], (BATCH, D), f32),
        "ada_w": nrm(ks[2], (L, D, 6 * D), 0.5 * D ** -0.5),
        "ada_b": nrm(ks[3], (L, 6 * D), 0.02),
        "norm1_g": gain(ks[4], (L, D)),
        "w_in": nrm(ks[5], (L, D, IN_WIDTH), D ** -0.5),
        "pool_w": nrm(ks[6], (L, N_POOL_GROUPS, POOL_GROUP, POOL_GROUP), POOL_GROUP ** -0.5),
        "pool_scale": gain(ks[7], (L, POOL_WIDTH)),
        "pool_out_g": gain(ks[8], (L, POOL_WIDTH)),
        "q_norm_g": gain(ks[9], (L, HEAD_DIM)),
        "k_norm_g": gain(ks[10], (L, HEAD_DIM)),
        "attn_out_g": gain(ks[11], (L, N_HEADS, HEAD_DIM)),
        "w_out": nrm(ks[12], (L, MIX_WIDTH, D), MIX_WIDTH ** -0.5),
        "norm2_g": gain(ks[13], (L, D)),
        "peer_wq": nrm(ks[14], (L, D, PEER_HEADS * PEER_QDIM), D ** -0.5),
        "peer_subkeys": nrm(ks[15], (L, PEER_HEADS, 2, PEER_KEYS, PEER_QDIM // 2), (PEER_QDIM // 2) ** -0.5),
        "peer_u": nrm(ks[16], (L, PEER_EXPERTS, D), D ** -0.5),
        "peer_v": nrm(ks[17], (L, PEER_EXPERTS, D), PEER_HEADS ** -0.5),
    }

def reference(x, c, ada_w, ada_b, norm1_g, w_in, pool_w, pool_scale, pool_out_g,
              q_norm_g, k_norm_g, attn_out_g, w_out, norm2_g, peer_wq, peer_subkeys,
              peer_u, peer_v):
    B, S, D = x.shape
    slopes = alibi_slopes(N_HEADS)
    cond = jax.nn.silu(c)
    for l in range(DEPTH):
        mod = (cond @ ada_w[l] + ada_b[l])[:, None, :]
        sh1, sc1, g1, sh2, sc2, g2 = jnp.split(mod, 6, axis=-1)

        h = rms_norm(x, norm1_g[l]) * (1 + sc1) + sh1
        proj = h @ w_in[l]
        u, q, k, v, qi, ki, wi = jnp.split(proj, IN_SPLITS, axis=-1)
        pool_out = pool_mixer(u, pool_w[l], pool_scale[l], pool_out_g[l])
        q = rms_norm(q.reshape(B, S, N_HEADS, HEAD_DIM), q_norm_g[l])
        k = rms_norm(k.reshape(B, S, N_HEADS, HEAD_DIM), k_norm_g[l])
        v = v.reshape(B, S, N_HEADS, HEAD_DIM)
        qi = qi.reshape(B, S, IDX_HEADS, IDX_DIM)
        wi = wi * (IDX_HEADS ** -0.5)
        attn = sparse_attention(q, k, v, qi, ki, wi, slopes)
        attn_out = rms_norm(attn, attn_out_g[l]).reshape(B, S, ATTN_WIDTH)
        mixed = jnp.concatenate([pool_out, attn_out], axis=-1) @ w_out[l]
        x = x + g1 * mixed

        h2 = rms_norm(x, norm2_g[l]) * (1 + sc2) + sh2
        x = x + g2 * peer_ffn(h2, peer_wq[l], peer_subkeys[l], peer_u[l], peer_v[l])
    return x


_drawn_inputs = setup_inputs


def setup_inputs(seed=0):
    import zlib

    import numpy as np

    out = dict(_drawn_inputs(seed))
    spreads = {}
    factors = {'pool_out_g': 2.667, 'q_norm_g': 4.266, 'k_norm_g': 4.186, 'norm2_g': 2.742}
    for name, (base, spread) in spreads.items():
        noise = np.random.default_rng([zlib.crc32(name.encode()), seed]).standard_normal(out[name].shape)
        drawn = base * np.exp(spread * noise) if base else spread * noise
        out[name] = __import__('jax').numpy.asarray(drawn.astype(out[name].dtype))
    for name, factor in factors.items():
        out[name] = (out[name] * factor).astype(out[name].dtype)
    return out
```

```python
from contextlib import ExitStack

import numpy as np

import concourse.bass as bass
from concourse import mybir

ALU = mybir.AluOpType
ACT = mybir.ActivationFunctionType
F32 = mybir.dt.float32
U32 = mybir.dt.uint32
AX_X = mybir.AxisListType.X

P = 128
D = 1024
KT = D // P
SEQ = 512
NT = SEQ // P
HEADS = 8
HD = 64
TOPK = 128
WIN = (2, 4, 8, 16)
EPS = 1e-6
MASKED = 1e30
TAKEN = -3e38
PH = 8
PK = 16
SLOTS = PH * PK
NB = 4
W_IN = 2632
IN_CHUNKS = 6
LAST = W_IN - 5 * 512
ITEMS = IN_CHUNKS * NT

R_C, R_ADAB, R_N1, R_N2, R_OG, R_QG, R_KG, NROWS = 0, 8, 56, 64, 72, 80, 81, 82
C_ID, C_DIST, C_IOTA, C_HK, NCST = 0, 128, 640, 656, 672
STEP_EVERY = 4
PIECES = 31


def constants():
    p = np.arange(P)[:, None].astype(np.float64)
    t = np.arange(P)[None, :].astype(np.float64)
    out = np.zeros((P, NCST + 12 * P))
    out[:, C_ID:C_ID + P] = p == t
    out[:, C_DIST:C_DIST + SEQ] = np.abs(p - (np.arange(SEQ)[None, :] - (SEQ - P)))
    out[:, C_IOTA:C_IOTA + 16] = np.arange(16)
    out[:, C_HK:C_HK + 8] = -(HD ** -0.5) * 2.0 ** np.arange(1, 9)
    out[:, C_HK + 8:C_HK + 16] = 1.0
    for g, w in enumerate(WIN):
        near = (p <= t) & (t - p < w)
        first = near / np.minimum(t + 1, w) - (p == t)
        later = near / w - (p == t)
        before = (t - (p - P) < w) / w
        for n, m in enumerate((first, later, before)):
            at = NCST + (n * 4 + g) * P
            out[:, at:at + P] = m
    return out.astype(np.float32)


def hymba_block(nc, x, c, ada_w, ada_b, norm1_g, w_in, pool_w, pool_scale, pool_out_g, q_norm_g,
                k_norm_g, attn_out_g, w_out, norm2_g, peer_wq, peer_subkeys, peer_u, peer_v, const,
                out):
    spill = nc.dram_tensor("spill", (NT, 3, P, SEQ), F32).ap()
    x2_dram = nc.dram_tensor("x2_dram", (SEQ, D), F32).ap()

    with ExitStack() as ctx:
        def sb(name, shape, dt=F32):
            return ctx.enter_context(nc.sbuf_tensor(name, shape, dt))

        def bank(name):
            return ctx.enter_context(nc.psum_tensor(name, [P, 512], F32))

        def sem(name):
            return ctx.enter_context(nc.semaphore(name))

        wq_sb = sb("wq_sb", [P, KT, 2048])
        wout_sb = sb("wout_sb", [P, KT, D])
        ring = sb("ring", [P, 2 * NB, D])
        keysT = sb("keysT", [P, 4, SEQ])
        vals = sb("vals", [P, NT, 512])
        kidxT = sb("kidxT", [P, SEQ])
        widx = sb("widx", [P, NT, 8])
        skT = sb("skT", [P, 16, P])
        tile_in = sb("tile_in", [P, 3, SEQ])
        front = sb("front", [P, 4, D])
        attT = sb("attT", [P, 512])
        gate2 = sb("gate2", [P, D])
        fin = sb("fin", [P, D])
        cst = sb("cst", [P, NCST])
        bias = sb("bias", [P, 512])
        score = sb("score", [P, 512])
        lg = sb("lg", [P, 2, 512])
        pr = sb("pr", [P, 2, 512])
        prT = sb("prT", [P, 2, 512])
        cols = sb("cols", [P, 96])
        modc = sb("modc", [P, 64])
        small = sb("small", [P, 128])
        topv = sb("topv", [P, 64])
        topi = sb("topi", [P, 64], U32)
        topf = sb("topf", [P, 64])
        wk = sb("wk", [P, 256])
        cval = sb("cval", [P, SLOTS])
        cpos = sb("cpos", [P, 32], U32)
        cpart = sb("cpart", [P, 2, 32], U32)
        csel = sb("csel", [P, 2, 32])
        eid = sb("eid", [P, 2, SLOTS], U32)
        gates = sb("gates", [P, 2, SLOTS])
        dots = sb("dots", [P, 2, PK])
        gel = sb("gel", [P, 2, PK])
        wts = sb("wts", [P, 2, PK])
        diag = sb("diag", [P, NB, P])
        gtmp = sb("gtmp", [P, 512])

        A = [bank("A0"), bank("A1")]
        T = [bank("T0"), bank("T1")]
        B = [bank("B0"), bank("B1")]
        acc = [bank("acc0"), bank("acc1")]

        ident = cst[:, C_ID:C_ID + P]
        xt = front[:, 0, :]
        h2T = front[:, 3, :]
        hT = front[:, :, :].rearrange("p a n -> p (a n)").rearrange("p (k t) -> p k t", k=KT)
        ubuf = [ring[:, b, :] for b in range(NB)]
        vbuf = [ring[:, NB + b, :] for b in range(NB)]

        room = wq_sb[:, :, :].rearrange("p k n -> p (k n)")
        x_all = room[:, 0:4096].rearrange("p (j n) -> p j n", j=NT)
        sk_raw = room[:, 0:2048].rearrange("p (b n) -> p b n", b=16)
        u_all = room[:, 8192:10240].rearrange("p (j n) -> p j n", j=NT)
        bands = room[:, 10240:11776].rearrange("p (b n) -> p b n", b=12)
        poolw = room[:, 11776:12288]
        pscale = room[:, 12288:12800]
        stage = room[:, 12800:14336].rearrange("p (b n) -> p b n", b=3)
        prm = room[:, 14336:14464]
        chunks = [ring[:, 0:4, :], ring[:, 4:8, :]]
        chunks = [a.rearrange("p a n -> p (a n)") for a in chunks] + [room[:, 4096:8192]]
        chunks = [a.rearrange("p (k n) -> p k n", k=KT) for a in chunks]
        square = pr
        normed = prT
        pooled_sb = lg[:, 0, :]
        pool_n = lg[:, 1, :]

        scol = modc[:, 0:8]
        a1, b1, a2, b2 = (modc[:, 8 + 8 * n:16 + 8 * n] for n in range(4))
        g1c, g2c, ecol = modc[:, 40:48], modc[:, 48:56], modc[:, 56:64]
        ss8, var8, y8, t8 = (small[:, 8 * n:8 * n + 8] for n in range(4))
        m8, mn8, rs8, rr8 = (small[:, 32 + 8 * n:40 + 8 * n] for n in range(4))
        ssx, gsum, grec = small[:, 64:68], small[:, 72:80], small[:, 80:88]
        sspool = small[:, 68:72]

        rows_in = sem("rows_in")
        cst_in = sem("cst_in")
        x_in = [sem(f"x_in{j}") for j in range(NT)]
        chunk_in = [sem(f"chunk_in{b}") for b in range(3)]
        pool_in = sem("pool_in")
        sk_in = sem("sk_in")
        wout_in = sem("wout_in")
        wq_in = [sem(f"wq_in{g}") for g in range(4)]
        tile_loaded = sem("tile_loaded")
        x2_saved = sem("x2_saved")
        fin_loaded = sem("fin_loaded")
        out_saved = sem("out_saved")
        spilled = [sem(f"spilled{b}") for b in range(3)]
        u_landed = [sem(f"u_landed{b}") for b in range(NB)]
        v_landed = [sem(f"v_landed{b}") for b in range(NB)]
        rowsT_ready = sem("rowsT_ready")
        cols_ready = sem("cols_ready")
        exp_c = sem("exp_c")
        scol_ready = sem("scol_ready")
        mod_ready = sem("mod_ready")
        mod_taken = sem("mod_taken")
        xss_ready = sem("xss_ready")
        xn_ready = sem("xn_ready")
        turned = sem("turned")
        turn_taken = sem("turn_taken")
        projected = sem("projected")
        item_squared = sem("item_squared")
        item_taken = [sem(f"item_taken{b}") for b in range(2)]
        normed_ready = [sem(f"normed_ready{b}") for b in range(2)]
        chunk_used = sem("chunk_used")
        poolw_ready = sem("poolw_ready")
        pooled = sem("pooled")
        pooled_taken = sem("pooled_taken")
        mixed = sem("mixed")
        mixed_squared = sem("mixed_squared")
        mixed_taken = sem("mixed_taken")
        stage_ready = sem("stage_ready")
        row_ready = sem("row_ready")
        row_taken = sem("row_taken")
        start_done = sem("start_done")
        dotted = sem("dotted")
        relu_done = sem("relu_done")
        relu_used = sem("relu_used")
        logits = sem("logits")
        biased = sem("biased")
        expd = sem("expd")
        probT = sem("probT")
        probT_taken = sem("probT_taken")
        pv_done = sem("pv_done")
        att_read = sem("att_read")
        att_ready = sem("att_ready")
        attT_ready = sem("attT_ready")
        attT_taken = sem("attT_taken")
        out_proj = sem("out_proj")
        x2_ready = sem("x2_ready")
        x2_squared = sem("x2_squared")
        xn2_ready = sem("xn2_ready")
        xn2T = sem("xn2T")
        h2T_ready = sem("h2T_ready")
        h2_turned = sem("h2_turned")
        h2_ready = sem("h2_ready")
        pq_done = sem("pq_done")
        pq_taken = sem("pq_taken")
        pscores = sem("pscores")
        pscores_taken = sem("pscores_taken")
        gate_in = sem("gate_in")
        gate_exp = sem("gate_exp")
        experts_ready = sem("experts_ready")
        u_used = sem("u_used")
        v_used = sem("v_used")
        gelu_done = sem("gelu_done")
        wts_ready = sem("wts_ready")
        diag_ready = sem("diag_ready")
        acc_taken = sem("acc_taken")
        fin_ready = sem("fin_ready")
        dve_step = sem("dve_step")
        act_step = sem("act_step")
        pool_step = sem("pool_step")

        stream = [("ada", a) for a in range(4)] + [("in", n) for n in range(IN_CHUNKS)] \
            + [("ada", a) for a in range(4, 12)]
        TURN_X = 2 * NT

        def width(ch):
            return 512 if ch < 5 else LAST

        def item(i):
            return i // NT, i % NT

        def is_turned(i):
            return 0 <= i < ITEMS and item(i)[0] in (1, 2, 4, 5)

        def normed_count(i):
            return sum(is_turned(m) for m in range(i % 2, i + 1, 2))

        def taken_before(i):
            return i // 2

        def pooled_at(i):
            return (i - 2) // 2 if i in (2, 4, 6, 8) else None

        def mix_at(i):
            return (i - 3) // 2 if i in (3, 5, 7, 9) else None

        def poolturn_at(i):
            return (i - 4) // 2 if i in (4, 6, 8, 10) else None

        turn_plan = []
        for i in range(ITEMS + 1):
            if is_turned(i - 1):
                turn_plan.append((item(i - 1)[0], item(i - 1)[1]))
            if poolturn_at(i) is not None:
                turn_plan.append(("pool", poolturn_at(i)))
        stage_plan = [("q", j) if ch == 1 else ("qi", j) if ch == 4 else ("pool", j)
                      for ch, j in turn_plan if ch in (1, 4, "pool")]
        SLAB = {"q": 0, "qi": 1, "pool": 2}
        TURNS = TURN_X + len(turn_plan) + 4

        IDX, TOP, ATT, END, PEER = 0, 8, 12, 22, 26
        ROUNDS = TOPK // 8 // 4

        def keys_of(j):
            return (j + 1) * P

        def step_piece(s):
            j, r = divmod(s, SLOTS)
            if j < NT - 1 and r % STEP_EVERY == 1 and r // STEP_EVERY < PIECES:
                return j + 1, r // STEP_EVERY
            return None

        block = ctx.enter_context(nc.Block())

        @block.sync
        def _(sp):
            rows = [(R_C, c.rearrange("a (r n) -> (a r) n", n=P), 8),
                    (R_ADAB, ada_b.rearrange("a (r n) -> (a r) n", n=P), 48),
                    (R_N1, norm1_g.rearrange("a (r n) -> (a r) n", n=P), 8),
                    (R_N2, norm2_g.rearrange("a (r n) -> (a r) n", n=P), 8),
                    (R_OG, pool_out_g.rearrange("a (r n) -> (a r) n", n=P), 4),
                    (R_OG + 4, attn_out_g.rearrange("a (r b) n -> (a r) (b n)", b=2), 4)]
            for at, src, n in rows:
                sp.dma_start(prm[at:at + n, :], src).then_inc(rows_in, 16)
            for half in range(2):
                for at, g in ((R_QG, q_norm_g), (R_KG, k_norm_g)):
                    sp.dma_start(prm[at:at + 1, half * HD:half * HD + HD], g).then_inc(rows_in, 16)
            sp.dma_start(cst[:, :], const[:, 0:NCST]).then_inc(cst_in, 16)
            sp.dma_start(x_all[:, 0, :], x[0, 0:P, :]).then_inc(x_in[0], 16)

            def load_chunk(n):
                kind, m = stream[n]
                if n >= 3:
                    sp.wait_ge(chunk_used, n - 2)
                if kind == "ada":
                    src, w = ada_w[0, :, m * 512:(m + 1) * 512], 512
                else:
                    src, w = w_in[0, :, m * 512:m * 512 + width(m)], width(m)
                sp.dma_start(chunks[n % 3][:, :, 0:w],
                             src.rearrange("(k p) n -> p k n", p=P)).then_inc(chunk_in[n % 3], 16)

            for n in range(3):
                load_chunk(n)
            for j in range(1, NT):
                sp.dma_start(x_all[:, j, :], x[0, j * P:(j + 1) * P, :]).then_inc(x_in[j], 16)
            load_chunk(3)
            sp.dma_start(bands, const[:, NCST:].rearrange("p (b n) -> p b n", b=12)).then_inc(pool_in, 16)
            sp.dma_start(poolw, pool_w[0].rearrange("g c d -> c g d")).then_inc(pool_in, 16)
            sp.dma_start(pscale, pool_scale[0:1, :].broadcast_to([P, 512])).then_inc(pool_in, 16)
            for n in range(4, 7):
                load_chunk(n)
            sp.dma_start(wout_sb[:, :, :], w_out[0].rearrange("(k p) n -> p k n", p=P)).then_inc(wout_in, 16)
            sp.wait_ge(turned, TURN_X)
            sp.dma_start(sk_raw, peer_subkeys[0].rearrange("h s n d -> n (h s) d")).then_inc(sk_in, 16)
            for n in range(7, len(stream)):
                load_chunk(n)

            def load_tile(j):
                if j == 0:
                    for b in range(3):
                        sp.wait_ge(spilled[b], 16 * len(stage_plan[b::3]))
                    sp.wait_ge(projected, ITEMS)
                else:
                    sp.wait_ge(out_proj, j)
                    sp.wait_ge(x2_saved, 16 * j)
                    sp.wait_ge(xn2_ready, j)
                    sp.wait_ge(x2_squared, j)
                sp.dma_start(tile_in[:, :, :], spill[j].rearrange("a p n -> p a n")).then_inc(tile_loaded, 16)
                sp.dma_start(xt, x[0, j * P:(j + 1) * P, :]).then_inc(tile_loaded, 16)

            load_tile(0)
            sp.wait_ge(start_done, 1)
            sp.wait_ge(chunk_used, len(stream))
            wq_v = peer_wq[0].rearrange("(k p) n -> p k n", p=P)
            for g in range(4):
                sp.dma_start(wq_sb[:, :, g * 512:(g + 1) * 512], wq_v[:, :, g * 512:(g + 1) * 512]).then_inc(wq_in[g], 16)

            def finish_tile(j):
                if j >= 1:
                    sp.wait_ge(out_saved, 16 * j)
                sp.dma_start(fin[:, :], x2_dram[j * P:(j + 1) * P, :]).then_inc(fin_loaded, 16)

            for j in range(NT):
                sp.wait_ge(x2_ready, j + 1)
                sp.dma_start(x2_dram[j * P:(j + 1) * P, :], xt).then_inc(x2_saved, 16)
                if j + 1 < NT:
                    load_tile(j + 1)
                if j >= 1:
                    sp.wait_ge(fin_ready, j)
                    sp.dma_start(out[0, (j - 1) * P:j * P, :], fin[:, :]).then_inc(out_saved, 16)
                if j == 0:
                    sp.wait_ge(x2_saved, 16)
                else:
                    sp.wait_ge(x2_saved, 16 * (j + 1))
                finish_tile(j)
            sp.wait_ge(fin_ready, NT)
            sp.dma_start(out[0, (NT - 1) * P:, :], fin[:, :]).then_inc(out_saved, 16)
            sp.wait_ge(out_saved, 16 * NT)

        @block.gpsimd
        def _(pool):
            for e, (what, j) in enumerate(stage_plan):
                pool.wait_ge(stage_ready, e + 1)
                pool.dma_start(spill[j, SLAB[what]], stage[:, e % 3, :]).then_inc(spilled[e % 3], 16)

            def gather(table, buf, landed, used, s):
                if s >= NB:
                    pool.wait_ge(used, s - NB + 1)
                    pool.wait_ge(landed[s % NB], 16 * (s // NB))
                j, r = divmod(s, SLOTS)
                pool.indirect_dma_start(
                    buf[s % NB], None, table,
                    bass.IndirectOffsetOnAxis(ap=eid[:, j % 2, r:r + 1], axis=0),
                ).then_inc(landed[s % NB], 16)

            pool.wait_ge(chunk_used, len(stream))
            for s in range(NT * SLOTS + PK):
                if s < NT * SLOTS:
                    if s % SLOTS == 0:
                        pool.wait_ge(experts_ready, s // SLOTS + 1)
                    gather(peer_u[0], ubuf, u_landed, u_used, s)
                if s >= PK:
                    gather(peer_v[0], vbuf, v_landed, v_used, s - PK)

        @block.tensor
        def _(pe):
            mm = nc.tensor.matmul
            pe.wait_ge(rows_in, 16 * 10)
            pe.wait_ge(cst_in, 16)
            nc.tensor.transpose(acc[1][:, 0:NROWS], prm[0:NROWS, :], ident[0:NROWS, 0:NROWS]).then_inc(rowsT_ready, 1)

            def chunk(n):
                pe.wait_ge(chunk_in[n % 3], 16 * (n // 3 + 1))
                return chunks[n % 3]

            def ada(n):
                w = chunk(n)
                a = stream[n][1]
                for b in range(4):
                    for k in range(KT):
                        last = mm(acc[0][:, 4 * a + b:4 * a + b + 1], w[:, k, b * P:(b + 1) * P],
                                  scol[:, k:k + 1], start=(k == 0), stop=(k == KT - 1))
                last.then_inc(chunk_used, 1)

            pe.wait_ge(scol_ready, 1)
            for n in range(4):
                ada(n)
            pe.drain().then_inc(mod_ready, 1) if False else None

            def turn_bank(n, src, blocks=4):
                if n >= 2:
                    pe.wait_ge(turn_taken, n - 1)
                for b in range(blocks):
                    last = nc.tensor.transpose(T[n % 2][:, b * P:(b + 1) * P], src[:, b * P:(b + 1) * P], ident)
                last.then_inc(turned, 1)

            for j in range(NT):
                pe.wait_ge(xn_ready, j + 1)
                for half in range(2):
                    turn_bank(2 * j + half, x_all[:, j, half * 512:(half + 1) * 512])

            turns = TURN_X
            for i in range(ITEMS + 1):
                if i < ITEMS:
                    ch, j = item(i)
                    w = chunk(4 + ch)
                    pe.wait_ge(turn_taken, 2 * j + 2)
                    if i >= 2:
                        pe.wait_ge(item_taken[i % 2], taken_before(i))
                    for k in range(KT):
                        last = mm(A[i % 2][:, 0:width(ch)], hT[:, k, j * P:(j + 1) * P], w[:, k, 0:width(ch)],
                                  start=(k == 0), stop=(k == KT - 1))
                    last.then_inc(projected, 1)
                    if j == NT - 1:
                        pe.wait_ge(projected, i + 1)
                        pe.sem_inc(chunk_used, 1)
                if is_turned(i - 1):
                    pe.wait_ge(normed_ready[(i - 1) % 2], normed_count(i - 1))
                    turn_bank(turns, normed[:, (i - 1) % 2, :], 1 if item(i - 1)[0] == 5 else 4)
                    turns += 1
                if (j := pooled_at(i)) is not None:
                    pe.wait_ge(pool_in, 48)
                    pe.wait_ge(item_taken[j % 2], j // 2 + 1)
                    if j >= 1:
                        pe.wait_ge(pooled_taken, j)
                    for g in range(4):
                        o = B[0][:, g * P:(g + 1) * P]
                        last = mm(o, u_all[:, j, g * P:(g + 1) * P], bands[:, g if j == 0 else 4 + g, :],
                                  start=True, stop=(j == 0))
                        if j >= 1:
                            last = mm(o, u_all[:, j - 1, g * P:(g + 1) * P], bands[:, 8 + g, :], start=False, stop=True)
                    last.then_inc(pooled, 1)
                if (j := mix_at(i)) is not None:
                    pe.wait_ge(pooled_taken, j + 1)
                    pe.wait_ge(poolw_ready, 1)
                    if j >= 1:
                        pe.wait_ge(mixed_taken, j)
                    for g in range(4):
                        last = mm(B[1][:, g * P:(g + 1) * P], pooled_sb[:, g * P:(g + 1) * P],
                                  poolw[:, g * P:(g + 1) * P], start=True, stop=True)
                    last.then_inc(mixed, 1)
                if (j := poolturn_at(i)) is not None:
                    pe.wait_ge(mixed_taken, j + 1)
                    turn_bank(turns, pool_n)
                    turns += 1
            pe.wait_ge(sk_in, 16)
            for g in range(4):
                turn_bank(turns, sk_raw[:, 4 * g:4 * g + 4, :].rearrange("p b n -> p (b n)"))
                turns += 1
            for n in range(10, len(stream)):
                ada(n)
            for r, col in enumerate((g1c, g2c)):
                pe.wait_ge(mod_taken, 2)
                if r == 0:
                    pe.wait_ge(item_taken[0], ITEMS // 2)
                    pe.wait_ge(item_taken[1], ITEMS // 2)
                else:
                    pe.wait_ge(row_taken, r)
                for b in range(KT):
                    last = mm(A[b // 4][:, (b % 4) * P:(b % 4 + 1) * P], col[:, b:b + 1].broadcast_to([P, P]),
                              ident, start=True, stop=True)
                last.then_inc(row_ready, 1)

            def front_piece(j, i):
                W = keys_of(j)
                qT, qiT, plT = (tile_in[:, n, :] for n in range(3))
                if i < TOP:
                    if j == 0:
                        return
                    if i == 0:
                        pe.wait_ge(tile_loaded, 32 * (j + 1))
                        pe.wait_ge(pscores_taken, 4 * j)
                    if i >= 2:
                        pe.wait_ge(relu_done, 8 * (j - 1) + i - 1)
                    o = HD * (i % 2)
                    mm(A[i % 2][:, 0:W], qiT[o:o + HD, (i // 2) * P:(i // 2 + 1) * P], kidxT[o:o + HD, 0:W],
                       start=True, stop=True).then_inc(dotted, 1)
                elif ATT <= i < END:
                    h = i - ATT
                    if h < HEADS:
                        if h == 0:
                            if j == 0:
                                pe.wait_ge(row_taken, 2)
                                pe.wait_ge(tile_loaded, 32)
                            else:
                                pe.wait_ge(relu_done, 8 * j)
                        if h >= 2:
                            pe.wait_ge(biased, 8 * j + h - 1)
                        o = HD * (h % 2)
                        mm(A[h % 2][:, 0:W], qT[o:o + HD, (h // 2) * P:(h // 2 + 1) * P], keysT[o:o + HD, h // 2, 0:W],
                           start=True, stop=True).then_inc(logits, 1)
                    if 1 <= h <= HEADS:
                        h -= 1
                        pe.wait_ge(expd, 8 * j + h + 1)
                        if h < 2:
                            pe.wait_ge(turn_taken, TURNS)
                            if j >= 1:
                                pe.wait_ge(h2_ready, 2 * j)
                        else:
                            pe.wait_ge(probT_taken, 8 * j + h - 1)
                        for b in range(j + 1):
                            last = nc.tensor.transpose(T[h % 2][:, b * P:(b + 1) * P], pr[:, h % 2, b * P:(b + 1) * P], ident)
                        last.then_inc(probT, 1)
                        h += 1
                    if h >= 2:
                        h -= 2
                        pe.wait_ge(probT_taken, 8 * j + h + 1)
                        if h == 0 and j >= 1:
                            pe.wait_ge(att_read, j)
                        for b in range(j + 1):
                            last = mm(B[0][:, h * HD:(h + 1) * HD], prT[:, h % 2, b * P:(b + 1) * P],
                                      vals[:, b, h * HD:(h + 1) * HD], start=(b == 0), stop=(b == j))
                        last.then_inc(pv_done, 1)
                elif i == END:
                    pe.wait_ge(att_ready, j + 1)
                    pe.wait_ge(probT_taken, 8 * j + 8)
                    for b in range(4):
                        last = nc.tensor.transpose(T[0][:, b * P:(b + 1) * P], score[:, b * P:(b + 1) * P], ident)
                    last.then_inc(attT_ready, 1)
                elif i == END + 1:
                    pe.wait_ge(attT_taken, j + 1)
                    pe.wait_ge(biased, 8 * j + 8)
                    pe.wait_ge(row_taken, 2)
                    for k in range(KT):
                        src = plT[:, k * P:(k + 1) * P] if k < 4 else attT[:, (k - 4) * P:(k - 3) * P]
                        for half in range(2):
                            last = mm(A[half][:, :], src, wout_sb[:, k, half * 512:(half + 1) * 512],
                                      start=(k == 0), stop=(k == KT - 1))
                    last.then_inc(out_proj, 1)
                elif i == END + 2:
                    pe.wait_ge(xn2_ready, j + 1)
                    for b in range(KT):
                        last = nc.tensor.transpose(T[b // 4][:, (b % 4) * P:(b % 4 + 1) * P],
                                                   front[:, 1 + j % 2, b * P:(b + 1) * P], ident)
                        if b % 4 == 3:
                            last.then_inc(xn2T, 1)
                elif i == END + 3:
                    for half in range(2):
                        pe.wait_ge(h2T_ready, 2 * j + half + 1)
                        for b in range(4):
                            k = 4 * half + b
                            last = nc.tensor.transpose(T[half][:, b * P:(b + 1) * P], h2T[:, k * P:(k + 1) * P], ident)
                        last.then_inc(h2_turned, 1)
                elif PEER <= i < PEER + 5:
                    g = i - PEER
                    if g < 4:
                        pe.wait_ge(wq_in[g], 16)
                        pe.wait_ge(h2T_ready, 2 * j + 2)
                        if 4 * j + g >= 1:
                            pe.wait_ge(pq_taken, 4 * j + g)
                        for b in range(4):
                            for k in range(KT):
                                last = mm(B[1][:, b * P:(b + 1) * P], wq_sb[:, k, (4 * g + b) * P:(4 * g + b + 1) * P],
                                          h2T[:, k * P:(k + 1) * P], start=(k == 0), stop=(k == KT - 1))
                        last.then_inc(pq_done, 1)
                    if g >= 1:
                        g -= 1
                        pe.wait_ge(pq_taken, 4 * j + g + 1)
                        if g < 2:
                            pe.wait_ge(x2_ready, j + 1)
                        else:
                            pe.wait_ge(pscores_taken, 4 * j + g - 1)
                        for b in range(4):
                            last = mm(A[g % 2][:, b * P:(b + 1) * P], prT[:, 0, b * P:(b + 1) * P],
                                      skT[:, 4 * g + b, :], start=True, stop=True)
                        last.then_inc(pscores, 1)

            for i in range(PIECES):
                front_piece(0, i)
            for s in range(NT * SLOTS + PK):
                m = s - PK
                if m >= 0:
                    j, r = divmod(m, SLOTS)
                    if r == 0 and j == 0:
                        pe.wait_ge(mod_taken, 2)
                    if r == 0 and j >= 1:
                        pe.wait_ge(acc_taken, j)
                    pe.wait_ge(diag_ready, m + 1)
                    pe.wait_ge(v_landed[m % NB], 16 * (m // NB + 1))
                    for half in range(2):
                        last = mm(acc[half][:, :], diag[:, m % NB, :], vbuf[m % NB][:, half * 512:(half + 1) * 512],
                                  start=(r == 0), stop=(r == SLOTS - 1))
                    last.then_inc(v_used, 1)
                if (piece := step_piece(s)) is not None:
                    front_piece(*piece)

        @block.scalar
        def _(act):
            steps = [0]

            def link(ins):
                steps[0] += 1
                ins.then_inc(act_step, 1)
                act.wait_ge(act_step, steps[0])

            fn = nc.scalar.activation
            act.wait_ge(cols_ready, 1)
            fn(ecol, cols[:, R_C:R_C + 8], ACT.Exp, scale=-1.0).then_inc(exp_c, 1)
            for j in range(NT):
                act.wait_ge(x_in[j], 16)
                if j >= 1:
                    act.wait_ge(xss_ready, j)
                fn(u_all[:, 0:2, :].rearrange("p a n -> p (a n)"), x_all[:, j, :], ACT.Square,
                   accum_out=ssx[:, j:j + 1]).then_inc(xss_ready, 1)
            act.wait_ge(xss_ready, NT)
            for i in range(ITEMS):
                ch, j = item(i)
                act.wait_ge(projected, i + 1)
                src = A[i % 2][:, 0:512]
                if ch == 0:
                    fn(u_all[:, j, :], src, ACT.Copy).then_inc(item_taken[i % 2], 1)
                elif ch in (1, 2):
                    if normed_count(i) > 1:
                        act.wait_ge(normed_ready[i % 2], normed_count(i) - 1)
                    fn(square[:, i % 2, :], src, ACT.Square).then_inc(item_squared, 1)
                elif ch == 3:
                    fn(vals[:, j, :], src, ACT.Copy).then_inc(item_taken[i % 2], 1)
                elif ch == 4:
                    act.wait_ge(turned, TURN_X + sum(1 for m in range(i - 1) if is_turned(m)) + NT)
                    act.wait_ge(normed_ready[i % 2], normed_count(i) - 1)
                    fn(normed[:, i % 2, :], src, ACT.Copy).then_inc(normed_ready[i % 2], 1)
                    act.wait_ge(normed_ready[i % 2], normed_count(i))
                    act.sem_inc(item_taken[i % 2], 1)
                if (t := pooled_at(i)) is not None:
                    act.wait_ge(pooled, t + 1)
                    if t >= 1:
                        act.wait_ge(mixed_taken, t)
                    fn(pooled_sb, B[0][:, :], ACT.Copy).then_inc(pooled_taken, 1)
                if (t := mix_at(i)) is not None:
                    act.wait_ge(mixed, t + 1)
                    fn(pooled_sb, B[1][:, :], ACT.Square, accum_out=sspool[:, t:t + 1]).then_inc(mixed_squared, 1)

            def front_piece(j, i):
                W = keys_of(j)
                if i < TOP:
                    if j == 0:
                        return
                    n = 8 * (j - 1) + i
                    act.wait_ge(dotted, n + 1)
                    if i >= 2:
                        act.wait_ge(relu_used, n - 1)
                    else:
                        act.wait_ge(probT, 8 * j)
                        if n >= 2:
                            act.wait_ge(relu_used, n - 1)
                    fn(pr[:, i % 2, 0:W], A[i % 2][:, 0:W], ACT.Relu).then_inc(relu_done, 1)
                elif ATT <= i < END:
                    h = i - ATT
                    if h < HEADS:
                        n = 8 * j + h
                        act.wait_ge(biased, n + 1)
                        if n >= 2:
                            act.wait_ge(probT, n - 1)
                        if h < 2 and j >= 1:
                            act.wait_ge(relu_used, 8 * j)
                        fn(pr[:, h % 2, 0:W], lg[:, h % 2, 0:W], ACT.Exp, bias=mn8[:, h:h + 1], scale=-1.0,
                           accum_out=rs8[:, h:h + 1]).then_inc(expd, 1)
                    if 1 <= h <= HEADS:
                        n = 8 * j + h - 1
                        act.wait_ge(probT, n + 1)
                        if h - 1 < 2 and j >= 1:
                            act.wait_ge(pscores, 4 * j)
                        if n >= 2:
                            act.wait_ge(pv_done, n - 1)
                        fn(prT[:, (h - 1) % 2, 0:W], T[(h - 1) % 2][:, 0:W], ACT.Copy).then_inc(probT_taken, 1)
                elif i == END:
                    act.wait_ge(attT_ready, j + 1)
                    if j >= 1:
                        act.wait_ge(out_proj, j)
                    fn(attT[:, :], T[0][:, :], ACT.Copy).then_inc(attT_taken, 1)
                elif i == END + 1:
                    act.wait_ge(x2_ready, j + 1)
                    if j >= 1:
                        act.wait_ge(pq_done, 4 * j)
                    fn(h2T, xt, ACT.Square, accum_out=ssx[:, 0:1]).then_inc(x2_squared, 1)
                elif i == END + 3:
                    for half in range(2):
                        act.wait_ge(h2_turned, 2 * j + half + 1)
                        fn(front[:, 1 + j % 2, half * 512:(half + 1) * 512], T[half][:, :], ACT.Copy).then_inc(h2_ready, 1)
                elif PEER <= i < PEER + 4:
                    g = i - PEER
                    act.wait_ge(pq_done, 4 * j + g + 1)
                    if g == 0:
                        act.wait_ge(pv_done, 8 * j + 8)
                    else:
                        act.wait_ge(pscores, 4 * j + g)
                    fn(prT[:, 0, :], B[1][:, :], ACT.Copy).then_inc(pq_taken, 1)
                elif i == PEER + 4:
                    act.wait_ge(gate_in, j + 1)
                    g3 = gates[:, j % 2, :]
                    fn(g3, g3, ACT.Exp).then_inc(gate_exp, 1)

            for i in range(PIECES):
                front_piece(0, i)
            for s in range(NT * SLOTS + PK):
                m = s - PK
                n, k = divmod(s, PK)
                if k == 0 and n >= 1:
                    act.wait_ge(u_used, PK * n)
                    if n >= 3:
                        act.wait_ge(wts_ready, n - 2)
                    fn(gel[:, (n - 1) % 2, :], dots[:, (n - 1) % 2, :], ACT.Gelu).then_inc(gelu_done, 1)
                if m >= 0:
                    q = m // PK
                    act.wait_ge(wts_ready, q + 1)
                    if m >= NB:
                        act.wait_ge(v_used, m - NB + 1)
                    fn(diag[:, m % NB, :], ident, ACT.Copy, scale=wts[:, q % 2, k:k + 1]).then_inc(diag_ready, 1)
                if (piece := step_piece(s)) is not None:
                    front_piece(*piece)

        @block.vector
        def _(dve):
            steps = [0]
            v = nc.vector

            def link(ins):
                steps[0] += 1
                ins.then_inc(dve_step, 1)
                dve.wait_ge(dve_step, steps[0])

            def rsqrt(y, var, t):
                link(v.tensor_scalar(t.bitcast(U32), var.bitcast(U32), 1, None, ALU.logical_shift_right))
                link(v.tensor_scalar(y.bitcast(U32), t.bitcast(U32), -1.0, float(0x5F3759DF), ALU.mult, ALU.add))
                for _ in range(4):
                    link(v.tensor_tensor(t, y, y, ALU.mult))
                    link(v.scalar_tensor_tensor(out=t, in0=t, scalar=-0.5, in1=var, op0=ALU.mult, op1=ALU.mult))
                    link(v.scalar_tensor_tensor(out=y, in0=t, scalar=1.5, in1=y, op0=ALU.add, op1=ALU.mult))

            dve.wait_ge(rowsT_ready, 1)
            v.tensor_copy(cols[:, 0:NROWS], acc[1][:, 0:NROWS]).then_inc(cols_ready, 1)
            dve.wait_ge(exp_c, 1)
            dve.wait_ge(cols_ready, 1)
            link(v.tensor_scalar(ecol, ecol, 1.0, None, ALU.add))
            link(v.reciprocal(ecol, ecol))
            v.tensor_tensor(scol, ecol, cols[:, R_C:R_C + 8], ALU.mult).then_inc(scol_ready, 1)

            for j in range(NT):
                dve.wait_ge(xss_ready, j + 1)
                link(v.tensor_scalar(var8[:, j:j + 1], ssx[:, j:j + 1], 1.0 / D, EPS, ALU.mult, ALU.add))
                rsqrt(y8[:, j:j + 1], var8[:, j:j + 1], t8[:, j:j + 1])
                v.tensor_scalar(x_all[:, j, :], x_all[:, j, :], y8[:, j:j + 1], None, ALU.mult).then_inc(xn_ready, 1)

            dve.wait_ge(chunk_used, 4)
            link(v.tensor_tensor(b1, acc[0][:, 0:8], cols[:, R_ADAB:R_ADAB + 8], ALU.add))
            link(v.tensor_tensor(a1, acc[0][:, 8:16], cols[:, R_ADAB + 8:R_ADAB + 16], ALU.add))
            link(v.scalar_tensor_tensor(out=a1, in0=a1, scalar=1.0, in1=cols[:, R_N1:R_N1 + 8], op0=ALU.add, op1=ALU.mult))

            turns = 0
            for j in range(NT):
                for half in range(2):
                    dve.wait_ge(turned, turns + 1)
                    for b in range(4):
                        k = 4 * half + b
                        last = v.tensor_scalar(hT[:, k, j * P:(j + 1) * P], T[turns % 2][:, b * P:(b + 1) * P],
                                               a1[:, k:k + 1], b1[:, k:k + 1], ALU.mult, ALU.add)
                    last.then_inc(turn_taken, 1)
                    turns += 1
            dve.wait_ge(pool_in, 48)
            v.tensor_tensor(poolw, poolw, pscale, ALU.mult).then_inc(poolw_ready, 1)

            staged = [0]

            def take_turn(what, j):
                nonlocal turns
                dve.wait_ge(turned, turns + 1)
                src = T[turns % 2]
                if what == 2:
                    last = v.tensor_scalar(keysT[:, :, j * P:(j + 1) * P], src[:, :].rearrange("p (a n) -> p a n", a=4),
                                           cols[:, R_KG:R_KG + 1], None, ALU.mult)
                elif what == 5:
                    last = v.tensor_copy(kidxT[:, j * P:(j + 1) * P], src[:, 0:P])
                else:
                    e = staged[0]
                    if e >= 3:
                        dve.wait_ge(spilled[e % 3], 16 * (e // 3))
                    dst = stage[:, e % 3, :]
                    if what == 1:
                        last = v.tensor_scalar(dst, src[:, :], cols[:, R_QG:R_QG + 1], None, ALU.mult)
                    else:
                        last = v.tensor_copy(dst, src[:, :])
                    last.then_inc(stage_ready, 1)
                    staged[0] += 1
                    dve.wait_ge(stage_ready, staged[0])
                    last = None
                if last is None:
                    dve.sem_inc(turn_taken, 1)
                else:
                    last.then_inc(turn_taken, 1)
                turns += 1

            for i in range(ITEMS + 1):
                if i < ITEMS:
                    ch, j = item(i)
                    b = i % 2
                    if ch in (1, 2):
                        dve.wait_ge(item_squared, sum(1 for m in range(i + 1) if item(m)[0] in (1, 2)))
                        link(v.reduce_sum(ss8, square[:, b, :].rearrange("p (h n) -> p h n", h=8), AX_X))
                        link(v.tensor_scalar(var8, ss8, 1.0 / HD, EPS, ALU.mult, ALU.add))
                        rsqrt(y8, var8, t8)
                        link(v.tensor_tensor(y8, y8, cst[:, C_HK + 8 * (ch - 1):C_HK + 8 * ch], ALU.mult))
                        if normed_count(i) > 1:
                            dve.wait_ge(turned, turns if is_turned(i - 2) else turns)
                        v.tensor_tensor(normed[:, b, :].rearrange("p (h n) -> p h n", h=8),
                                        A[b][:, :].rearrange("p (h n) -> p h n", h=8),
                                        y8.unsqueeze(2).broadcast_to([P, 8, HD]), ALU.mult).then_inc(normed_ready[b], 1)
                        dve.wait_ge(normed_ready[b], normed_count(i))
                        dve.sem_inc(item_taken[b], 1)
                    elif ch == 5:
                        dve.wait_ge(projected, i + 1)
                        dve.wait_ge(turned, turns)
                        dve.wait_ge(normed_ready[b], normed_count(i) - 1)
                        v.tensor_copy(normed[:, b, 0:HD], A[b][:, 0:HD])
                        v.tensor_copy(normed[:, b, HD:P], A[b][:, 0:HD])
                        link(v.tensor_scalar(widx[:, j, :], A[b][:, HD:HD + 8], float(np.float32(8 ** -0.5)),
                                             HD ** -0.5, ALU.mult, ALU.mult))
                        dve.sem_inc(normed_ready[b], 1)
                        dve.sem_inc(item_taken[b], 1)
                if is_turned(i - 1):
                    take_turn(*item(i - 1))
                if (j := mix_at(i)) is not None:
                    dve.wait_ge(mixed_squared, j + 1)
                    link(v.tensor_scalar(var8[:, 0:1], sspool[:, j:j + 1], 1.0 / 512, EPS, ALU.mult, ALU.add))
                    rsqrt(y8[:, 0:1], var8[:, 0:1], t8[:, 0:1])
                    if j >= 1:
                        dve.wait_ge(turned, turns)
                    v.tensor_scalar(pool_n, B[1][:, :], y8[:, 0:1], None, ALU.mult).then_inc(mixed_taken, 1)
                    dve.wait_ge(mixed_taken, j + 1)
                if (j := poolturn_at(i)) is not None:
                    take_turn("pool", j)
            for g in range(4):
                dve.wait_ge(turned, turns + 1)
                v.tensor_copy(skT[:, 4 * g:4 * g + 4, :].rearrange("p a n -> p (a n)"), T[turns % 2][:, :])\
                    .then_inc(turn_taken, 1)
                turns += 1
            dve.wait_ge(turn_taken, TURNS)
            dve.wait_ge(chunk_used, len(stream))
            bias_of = cols[:, R_ADAB:R_ADAB + 48]
            link(v.tensor_tensor(g1c, acc[0][:, 16:24], bias_of[:, 16:24], ALU.add))
            link(v.tensor_tensor(g2c, acc[0][:, 40:48], bias_of[:, 40:48], ALU.add))
            link(v.tensor_tensor(b2, acc[0][:, 24:32], bias_of[:, 24:32], ALU.add))
            link(v.tensor_tensor(a2, acc[0][:, 32:40], bias_of[:, 32:40], ALU.add))
            link(v.scalar_tensor_tensor(out=a2, in0=a2, scalar=1.0, in1=cols[:, R_N2:R_N2 + 8], op0=ALU.add, op1=ALU.mult))
            dve.sem_inc(mod_taken, 2)
            dve.sem_inc(start_done, 1)
            dve.wait_ge(row_ready, 1)
            dve.wait_ge(wout_in, 16)
            for k in range(KT):
                for half in range(2):
                    w = wout_sb[:, k, half * 512:(half + 1) * 512]
                    last = v.scalar_tensor_tensor(out=w, in0=w, scalar=cols[:, R_OG + k:R_OG + k + 1], in1=A[half][:, :],
                                                  op0=ALU.mult, op1=ALU.mult)
            last.then_inc(row_taken, 1)
            dve.wait_ge(row_ready, 2)
            v.tensor_copy(gate2[:, 0:512], A[0][:, :])
            v.tensor_copy(gate2[:, 512:1024], A[1][:, :]).then_inc(row_taken, 1)

            def front_piece(j, i):
                W = keys_of(j)
                if i < TOP:
                    if j == 0:
                        return
                    n = 8 * (j - 1) + i
                    if i == 0:
                        dve.wait_ge(attT_ready, j)
                    else:
                        dve.wait_ge(relu_used, n)
                    dve.wait_ge(relu_done, n + 1)
                    w = widx[:, j, i:i + 1]
                    if i == 0:
                        v.tensor_scalar(score[:, 0:W], pr[:, 0, 0:W], w, None, ALU.mult).then_inc(relu_used, 1)
                    else:
                        v.scalar_tensor_tensor(out=score[:, 0:W], in0=pr[:, i % 2, 0:W], scalar=w, in1=score[:, 0:W],
                                               op0=ALU.mult, op1=ALU.add).then_inc(relu_used, 1)
                elif i < ATT:
                    dist = cst[:, C_DIST + SEQ - W:C_DIST + SEQ]
                    if j == 0:
                        if i == TOP:
                            link(v.tensor_copy(bias[:, 0:W], dist))
                            link(v.memset(bias[0:HD, W - HD:W], MASKED))
                        return
                    if i == TOP:
                        dve.wait_ge(relu_used, 8 * j)
                        link(v.memset(score[0:HD, W - HD:W], -MASKED))
                    for _ in range(ROUNDS):
                        link(v.max(m8, score[:, 0:W]))
                        link(v.match_replace(out=score[:, 0:W], in_to_replace=m8, in_values=score[:, 0:W], imm_value=TAKEN))
                    if i == ATT - 1:
                        dve.wait_ge(biased, 8 * j)
                        link(v.tensor_scalar(score[:, 0:W], score[:, 0:W], -2e38, MASKED, ALU.is_gt, ALU.mult))
                        link(v.tensor_tensor(bias[:, 0:W], score[:, 0:W], dist, ALU.add))
                elif ATT <= i < END:
                    h = i - ATT
                    if h < HEADS:
                        n = 8 * j + h
                        dve.wait_ge(logits, n + 1)
                        if n >= 2:
                            dve.wait_ge(expd, n - 1)
                        if h == 0 and j >= 1:
                            dve.wait_ge(expd, 8 * j)
                        v.tensor_tensor_reduce(out=lg[:, h % 2, 0:W], in0=bias[:, 0:W], in1=A[h % 2][:, 0:W],
                                               scale=2.0 ** -(h + 1), scalar=3e38, op0=ALU.add, op1=ALU.min,
                                               accum_out=mn8[:, h:h + 1]).then_inc(biased, 1)
                elif i == END:
                    dve.wait_ge(pv_done, 8 * j + 8)
                    dve.wait_ge(biased, 8 * j + 8)
                    o3 = score[:, :].rearrange("p (h n) -> p h n", h=8)
                    sq = lg[:, 0, :]
                    link(v.reciprocal(rr8, rs8))
                    v.tensor_tensor(o3, B[0][:, :].rearrange("p (h n) -> p h n", h=8),
                                    rr8.unsqueeze(2).broadcast_to([P, 8, HD]), ALU.mult).then_inc(att_read, 1)
                    dve.wait_ge(att_read, j + 1)
                    link(v.tensor_tensor(sq, score[:, :], score[:, :], ALU.mult))
                    link(v.reduce_sum(ss8, sq.rearrange("p (h n) -> p h n", h=8), AX_X))
                    link(v.tensor_scalar(var8, ss8, 1.0 / HD, EPS, ALU.mult, ALU.add))
                    rsqrt(y8, var8, t8)
                    v.tensor_tensor(o3, o3, y8.unsqueeze(2).broadcast_to([P, 8, HD]), ALU.mult).then_inc(att_ready, 1)
                elif i == END + 1:
                    dve.wait_ge(tile_loaded, 32 * (j + 1))
                    dve.wait_ge(out_proj, j + 1)
                    v.tensor_tensor(xt[:, 0:512], xt[:, 0:512], A[0][:, :], ALU.add)
                    v.tensor_tensor(xt[:, 512:1024], xt[:, 512:1024], A[1][:, :], ALU.add).then_inc(x2_ready, 1)
                elif i == END + 2:
                    dve.wait_ge(x2_squared, j + 1)
                    link(v.tensor_scalar(var8[:, 0:1], ssx[:, 0:1], 1.0 / D, EPS, ALU.mult, ALU.add))
                    rsqrt(y8[:, 0:1], var8[:, 0:1], t8[:, 0:1])
                    if j >= 2:
                        dve.wait_ge(u_used, SLOTS * (j - 1))
                    v.tensor_scalar(front[:, 1 + j % 2, :], xt, y8[:, 0:1], None, ALU.mult).then_inc(xn2_ready, 1)
                elif i == END + 3:
                    for half in range(2):
                        dve.wait_ge(xn2T, 2 * j + half + 1)
                        for b in range(4):
                            k = 4 * half + b
                            last = v.tensor_scalar(h2T[:, k * P:(k + 1) * P], T[half][:, b * P:(b + 1) * P],
                                                   a2[:, k:k + 1], b2[:, k:k + 1], ALU.mult, ALU.add)
                        last.then_inc(h2T_ready, 1)
                elif PEER + 1 <= i < PEER + 5:
                    g = i - PEER - 1
                    peer_top(j, g)
                    if g == 3:
                        gate_softmax(j)

            def top16(vals16, idx16, src):
                w = wk[:, 0:src.shape[-1]]
                link(v.max(vals16[:, 0:8], src))
                link(v.match_replace(out=w, in_to_replace=vals16[:, 0:8], in_values=src, imm_value=TAKEN))
                link(v.max_index(idx16[:, 0:8], vals16[:, 0:8], src))
                link(v.max(vals16[:, 8:16], w))
                link(v.max_index(idx16[:, 8:16], vals16[:, 8:16], w))

            def peer_top(j, g):
                dve.wait_ge(pscores, 4 * j + g + 1)
                for b in range(4):
                    top16(topv[:, 16 * b:16 * b + 16], topi[:, 16 * b:16 * b + 16], A[g % 2][:, b * P:(b + 1) * P])
                dve.sem_inc(pscores_taken, 1)
                link(v.tensor_copy(topf[:, :], topi[:, :]))
                cand = lg[:, 0, :]
                one = lg[:, 1, :].rearrange("p (a b) -> p a b", b=16)
                for h in range(2):
                    f = topv[:, 32 * h:32 * h + 16].unsqueeze(2).broadcast_to([P, 16, 16])
                    s = topv[:, 32 * h + 16:32 * h + 32].unsqueeze(1).broadcast_to([P, 16, 16])
                    link(v.tensor_tensor(cand[:, 256 * h:256 * h + 256].rearrange("p (a b) -> p a b", b=16), f, s, ALU.add))
                    at = 16 * (2 * g + h)
                    top16(cval[:, at:at + 16], cpos[:, 16 * h:16 * h + 16], cand[:, 256 * h:256 * h + 256])
                link(v.tensor_scalar(cpart[:, 0, :], cpos[:, :], 4, None, ALU.logical_shift_right))
                link(v.tensor_scalar(cpart[:, 1, :], cpos[:, :], 15, None, ALU.bitwise_and))
                iota = cst[:, C_IOTA:C_IOTA + 16].unsqueeze(1).broadcast_to([P, 32, 16])
                for side in range(2):
                    link(v.tensor_tensor(one, cpart[:, side, :].unsqueeze(2).broadcast_to([P, 32, 16]), iota, ALU.is_equal))
                    for h in range(2):
                        key = topf[:, 32 * h + 16 * side:32 * h + 16 * side + 16].unsqueeze(1).broadcast_to([P, 16, 16])
                        link(v.tensor_tensor(one[:, 16 * h:16 * h + 16, :], one[:, 16 * h:16 * h + 16, :], key, ALU.mult))
                    link(v.reduce_sum(csel[:, side, :], one, AX_X))
                link(v.scalar_tensor_tensor(out=eid[:, j % 2, 32 * g:32 * g + 32], in0=csel[:, 0, :], scalar=128.0,
                                            in1=csel[:, 1, :], op0=ALU.mult, op1=ALU.add))

            def gate_softmax(j):
                g3 = gates[:, j % 2, :].rearrange("p (h k) -> p h k", h=PH)
                c3 = cval[:, :].rearrange("p (h k) -> p h k", h=PH)
                v.tensor_tensor(g3, c3, c3[:, :, 0:1].broadcast_to([P, PH, PK]), ALU.subtract).then_inc(gate_in, 1)
                dve.wait_ge(gate_exp, j + 1)
                link(v.reduce_sum(gsum, g3, AX_X))
                link(v.reciprocal(grec, gsum))
                dve.wait_ge(h2_ready, 2 * j + 2)
                link(v.tensor_tensor(g3, g3, grec.unsqueeze(2).broadcast_to([P, PH, PK]), ALU.mult))
                dve.sem_inc(experts_ready, 1)

            for i in range(PIECES):
                front_piece(0, i)
            for s in range(NT * SLOTS + PK + 1):
                n, k = divmod(s, PK)
                if s < NT * SLOTS:
                    j = s // SLOTS
                    dve.wait_ge(u_landed[s % NB], 16 * (s // NB + 1))
                    if k == 0 and n >= 2:
                        dve.wait_ge(gelu_done, n - 1)
                    buf = ubuf[s % NB]
                    v.scalar_tensor_tensor(out=buf, in0=buf, scalar=1.0, in1=front[:, 1 + j % 2, :], op0=ALU.mult,
                                           op1=ALU.mult, accum_out=dots[:, n % 2, k:k + 1]).then_inc(u_used, 1)
                if k == 1 and 1 <= n <= NT * PH:
                    m = n - 1
                    dve.wait_ge(gelu_done, m + 1)
                    if m >= 2:
                        dve.wait_ge(diag_ready, PK * (m - 1))
                    h = m % PH
                    v.tensor_tensor(wts[:, m % 2, :], gel[:, m % 2, :], gates[:, (m // PH) % 2, h * PK:(h + 1) * PK],
                                    ALU.mult).then_inc(wts_ready, 1)
                r = s - PK
                if r >= SLOTS and r % SLOTS == 0:
                    j = r // SLOTS - 1
                    dve.wait_ge(v_used, SLOTS * (j + 1))
                    dve.wait_ge(fin_loaded, 16 * (j + 1))
                    for half in range(2):
                        cut = slice(half * 512, (half + 1) * 512)
                        link(v.tensor_tensor(gtmp[:, :], acc[half][:, :], gate2[:, cut], ALU.mult))
                        link(v.tensor_tensor(fin[:, cut], fin[:, cut], gtmp[:, :], ALU.add))
                    dve.sem_inc(acc_taken, 1)
                    dve.sem_inc(fin_ready, 1)
                if (piece := step_piece(s)) is not None:
                    front_piece(*piece)


_INS = ["x", "c", "ada_w", "ada_b", "norm1_g", "w_in", "pool_w", "pool_scale", "pool_out_g", "q_norm_g",
        "k_norm_g", "attn_out_g", "w_out", "norm2_g", "peer_wq", "peer_subkeys", "peer_u", "peer_v"]


def kernel(**inputs):
    import numpy as _np
    import concourse.bacc as _bacc
    from concourse import mybir as _mybir
    from concourse.bass_utils import run_bass_kernel_spmd as _run

    nc = _bacc.Bacc("TRN2", target_bir_lowering=False, num_devices=1, dynamic_dma_scratch_size=8192)
    arrays, args = {}, []
    for name in _INS + ["const"]:
        a = constants() if name == "const" else _np.ascontiguousarray(inputs[name])
        arrays[f"in_{name}"] = a
        args.append(nc.dram_tensor(f"in_{name}", a.shape, _mybir.dt.from_np(a.dtype), kind="ExternalInput").ap())
    out = nc.dram_tensor("out_0", (1, SEQ, D), F32, kind="ExternalOutput").ap()
    hymba_block(nc, *args, out)
    r = _run(nc, [arrays], core_ids=[0])
    return r.results[0]["out_0"]
```

```python
from contextlib import ExitStack

import numpy as np

import concourse.bass as bass
from concourse import mybir

ALU = mybir.AluOpType
ACT = mybir.ActivationFunctionType
F32 = mybir.dt.float32
U32 = mybir.dt.uint32
AX_X = mybir.AxisListType.X

P = 128
D = 1024
KT = D // P
SEQ = 512
NT = SEQ // P
HEADS = 8
HD = 64
TOPK = 128
WIN = (2, 4, 8, 16)
EPS = 1e-6
MASKED = 1e30
TAKEN = -3e38
PH = 8
PK = 16
SLOTS = PH * PK
NB = 4
W_IN = 2632
IN_CHUNKS = 6
IN_ORDER = (0, 1, 2, 5, 4, 3)
LAST = W_IN - 5 * 512
ITEMS = IN_CHUNKS * NT

R_C, R_ADAB, R_N1, R_N2, R_OG, R_QG, R_KG, NROWS = 0, 8, 56, 64, 72, 80, 81, 82
C_ID, C_DIST, C_IOTA, C_HK, NCST = 0, 128, 640, 656, 672
IDX, TOP, ATT, END, PEER, PIECES = 0, 9, 26, 36, 46, 67
ATT_TURN, OUT_PROJ, X2, XN2, H2T, H2 = END + 1, END + 2, END + 6, END + 7, END + 8, END + 9
SPLIT = PEER + 9
WEIGHT = [5] * TOP + [8] * (ATT - TOP) + [10] * (END - ATT) + [14] * (PEER - END) + [16] * (PIECES - PEER)


def constants():
    p = np.arange(P)[:, None].astype(np.float64)
    t = np.arange(P)[None, :].astype(np.float64)
    out = np.zeros((P, NCST + 12 * P))
    out[:, C_ID:C_ID + P] = p == t
    out[:, C_DIST:C_DIST + SEQ] = np.abs(p - (np.arange(SEQ)[None, :] - (SEQ - P)))
    out[:, C_IOTA:C_IOTA + 16] = np.arange(16)
    out[:, C_HK:C_HK + 8] = -(HD ** -0.5) * 2.0 ** np.arange(1, 9)
    out[:, C_HK + 8:C_HK + 16] = 1.0
    for g, w in enumerate(WIN):
        near = (p <= t) & (t - p < w)
        first = near / np.minimum(t + 1, w) - (p == t)
        later = near / w - (p == t)
        before = (t - (p - P) < w) / w
        for n, m in enumerate((first, later, before)):
            at = NCST + (n * 4 + g) * P
            out[:, at:at + P] = m
    return out.astype(np.float32)


def hymba_block(nc, x, c, ada_w, ada_b, norm1_g, w_in, pool_w, pool_scale, pool_out_g, q_norm_g,
                k_norm_g, attn_out_g, w_out, norm2_g, peer_wq, peer_subkeys, peer_u, peer_v, const,
                out):
    spill = nc.dram_tensor("spill", (NT, 3, P, SEQ), F32).ap()
    x2_dram = nc.dram_tensor("x2_dram", (SEQ, D), F32).ap()

    with ExitStack() as ctx:
        def sb(name, shape, dt=F32):
            return ctx.enter_context(nc.sbuf_tensor(name, shape, dt))

        def bank(name):
            return ctx.enter_context(nc.psum_tensor(name, [P, 512], F32))

        def sem(name):
            return ctx.enter_context(nc.semaphore(name))

        wq_sb = sb("wq_sb", [P, 4, KT, 512])
        wout_sb = sb("wout_sb", [P, KT, D])
        ring = sb("ring", [P, 2 * NB, D])
        keysT = sb("keysT", [P, 4, SEQ])
        vals = sb("vals", [P, NT, 512])
        kidxT = sb("kidxT", [P, SEQ])
        widx = sb("widx", [P, NT, 8])
        skT = sb("skT", [P, 16, P])
        tile_in = sb("tile_in", [P, 3, SEQ])
        front = sb("front", [P, 4, D])
        attT = sb("attT", [P, 512])
        gate2 = sb("gate2", [P, D])
        fin = sb("fin", [P, D])
        cst = sb("cst", [P, NCST])
        bias = sb("bias", [P, 512])
        score = sb("score", [P, 512])
        lg = sb("lg", [P, 2, 512])
        pr = sb("pr", [P, 2, 512])
        prT = sb("prT", [P, 2, 512])
        cols = sb("cols", [P, 96])
        modc = sb("modc", [P, 64])
        small = sb("small", [P, 128])
        topv = sb("topv", [P, 64])
        topi = sb("topi", [P, 64], U32)
        topf = sb("topf", [P, 64])
        wk = sb("wk", [P, 512])
        cval = sb("cval", [P, SLOTS])
        cpos = sb("cpos", [P, 32], U32)
        cpart = sb("cpart", [P, 2, 32], U32)
        csel = sb("csel", [P, 2, 32])
        eid = sb("eid", [P, 2, SLOTS], U32)
        gates = sb("gates", [P, 2, SLOTS])
        dots = sb("dots", [P, 2, PK])
        gel = sb("gel", [P, 2, PK])
        wts = sb("wts", [P, 2, PK])
        diag = sb("diag", [P, NB, P])

        A = [bank("A0"), bank("A1")]
        T = [bank("T0"), bank("T1")]
        B = [bank("B0"), bank("B1")]
        acc = [bank("acc0"), bank("acc1")]

        ident = cst[:, C_ID:C_ID + P]
        xt = front[:, 0, :]
        h2T = front[:, 3, :]
        hT = front[:, :, :].rearrange("p a n -> p (a n)").rearrange("p (k t) -> p k t", k=KT)
        ubuf = [ring[:, b, :] for b in range(NB)]
        vbuf = [ring[:, NB + b, :] for b in range(NB)]

        room = wq_sb[:, :, :, :].rearrange("p g k n -> p (g k n)")
        x_all = room[:, 0:4096].rearrange("p (j n) -> p j n", j=NT)
        sk_raw = room[:, 0:2048].rearrange("p (b n) -> p b n", b=16)
        u_all = room[:, 8192:10240].rearrange("p (j n) -> p j n", j=NT)
        bands = room[:, 10240:11776].rearrange("p (b n) -> p b n", b=12)
        poolw = room[:, 11776:12288]
        pscale = room[:, 12288:12800]
        stage = room[:, 12800:14336].rearrange("p (b n) -> p b n", b=3)
        prm = room[:, 14336:14464]
        partial = room[:, 14464:15488].rearrange("p (b n) -> p b n", b=2)
        modcol = acc[1][:, 128:176]
        chunks = [ring[:, 0:4, :], ring[:, 4:8, :]]
        chunks = [a.rearrange("p a n -> p (a n)") for a in chunks] + [room[:, 4096:8192]]
        chunks = [a.rearrange("p (k n) -> p k n", k=KT) for a in chunks]
        chunks.append(fin[:, 0:KT * LAST].rearrange("p (k n) -> p k n", k=KT))
        square = pr
        normed = prT
        pooled_sb = lg[:, 0, :]
        pool_n = lg[:, 1, :]

        ones = sb("ones", [P, 1])
        scol = modc[:, 0:8]
        a1, b1, a2, b2 = (modc[:, 8 + 8 * n:16 + 8 * n] for n in range(4))
        g1c, g2c, ecol = modc[:, 40:48], modc[:, 48:56], modc[:, 56:64]
        ss8, var8, y8, t8 = (small[:, 8 * n:8 * n + 8] for n in range(4))
        m8, mn8, rs8, rr8 = (small[:, 32 + 8 * n:40 + 8 * n] for n in range(4))
        ssx, gsum, grec = small[:, 64:68], small[:, 72:80], small[:, 80:88]
        sspool = small[:, 68:72]

        rows_in = sem("rows_in")
        cst_in = sem("cst_in")
        x_in = [sem(f"x_in{j}") for j in range(NT)]
        chunk_in = [sem(f"chunk_in{b}") for b in range(4)]
        pool_in = sem("pool_in")
        sk_in = sem("sk_in")
        wout_in = sem("wout_in")
        wq_in = [sem(f"wq_in{g}") for g in range(4)]
        tile_loaded = sem("tile_loaded")
        xt_loaded = sem("xt_loaded")
        x2_saved = sem("x2_saved")
        fin_loaded = sem("fin_loaded")
        out_saved = sem("out_saved")
        spilled = [sem(f"spilled{b}") for b in range(3)]
        u_landed = [sem(f"u_landed{b}") for b in range(NB)]
        v_landed = [sem(f"v_landed{b}") for b in range(NB)]
        rowsT_ready = sem("rowsT_ready")
        cols_ready = sem("cols_ready")
        exp_c = sem("exp_c")
        scol_ready = sem("scol_ready")
        mod_taken = sem("mod_taken")
        xss_ready = sem("xss_ready")
        xn_ready = sem("xn_ready")
        turned = sem("turned")
        turn_taken = sem("turn_taken")
        projected = sem("projected")
        item_squared = sem("item_squared")
        item_taken = [sem(f"item_taken{b}") for b in range(2)]
        normed_ready = [sem(f"normed_ready{b}") for b in range(2)]
        partial_ready = [sem(f"partial_ready{b}") for b in range(2)]
        modcol_ready = sem("modcol_ready")
        poolw_ready = sem("poolw_ready")
        pooled = sem("pooled")
        pooled_taken = sem("pooled_taken")
        mixed = sem("mixed")
        mixed_squared = sem("mixed_squared")
        mixed_taken = sem("mixed_taken")
        row_ready = sem("row_ready")
        row_taken = sem("row_taken")
        dotted = sem("dotted")
        relu_done = sem("relu_done")
        relu_used = sem("relu_used")
        logits = sem("logits")
        biased = sem("biased")
        expd = sem("expd")
        probT = sem("probT")
        probT_taken = sem("probT_taken")
        pv_done = sem("pv_done")
        att_read = sem("att_read")
        att_ready = sem("att_ready")
        attT_ready = sem("attT_ready")
        attT_taken = sem("attT_taken")
        out_proj = sem("out_proj")
        x2_ready = sem("x2_ready")
        x2_squared = sem("x2_squared")
        xn2_ready = sem("xn2_ready")
        xn2T = sem("xn2T")
        h2T_ready = sem("h2T_ready")
        h2_turned = sem("h2_turned")
        h2_ready = sem("h2_ready")
        pq_done = sem("pq_done")
        pq_taken = sem("pq_taken")
        pscores = sem("pscores")
        pscores_taken = sem("pscores_taken")
        gate_in = sem("gate_in")
        gate_exp = sem("gate_exp")
        experts_ready = sem("experts_ready")
        u_used = sem("u_used")
        v_used = sem("v_used")
        gelu_done = sem("gelu_done")
        wts_ready = sem("wts_ready")
        diag_ready = sem("diag_ready")
        fin_ready = sem("fin_ready")
        dve_step = sem("dve_step")
        act_step = sem("act_step")
        pool_step = sem("pool_step")

        stream = [("ada", 0, 2), ("ada", 1, 0), ("ada", 2, 1), ("ada", 3, 2), ("in", 0, 0), ("in", 1, 1),
                  ("ada", 4, 2), ("in", 3, 3), ("ada", 5, 2), ("in", 2, 0), ("ada", 6, 2), ("in", 4, 1),
                  ("ada", 7, 2), ("ada", 8, 2), ("in", 5, 0), ("ada", 9, 2), ("ada", 10, 2), ("ada", 11, 2)]
        in_buffer = {b: [(kind, m) for kind, m, o in stream if o == b] for b in range(4)}
        at_stream = {(kind, m): (b, in_buffer[b].index((kind, m)) + 1) for kind, m, b in stream}
        BY_POOL = (1, 6, 7)
        DVE_ADA_AT = {0: 4, 1: 5, 11: 8, 15: 9, 17: 10, 18: 11}
        ADA_AT = {2: 4, 3: 5, 8: 6, 11: 7, 15: 8, 16: 9, 18: 10, 19: 11}
        MODS_AT = 19
        ROW_AT = 20
        TURN_X = 2 * NT

        def width(ch):
            return 512 if ch < 5 else LAST

        def item(i):
            return IN_ORDER[i // NT], i % NT

        def chunk_loaded(eng, kind, m):
            b, count = at_stream[kind, m]
            eng.wait_ge(chunk_in[b], 16 * count)
            return chunks[b]

        def partial_made(eng, a):
            eng.wait_ge(partial_ready[a % 2], a // 2 + 1)

        def is_turned(i):
            return 0 <= i < ITEMS and item(i)[0] in (1, 2, 4, 5)

        def normed_count(i):
            return sum(is_turned(m) for m in range(i % 2, i + 1, 2))

        def taken_count(i):
            return sum(item(m)[0] in (0, 3) for m in range(i % 2, i + 1, 2))

        def item_left(eng, i):
            if is_turned(i):
                eng.wait_ge(normed_ready[i % 2], normed_count(i))
            else:
                eng.wait_ge(item_taken[i % 2], taken_count(i))

        def pooled_at(i):
            return (i - 2) // 2 if i in (2, 4, 6, 8) else None

        def mix_at(i):
            return (i - 3) // 2 if i in (3, 5, 7, 9) else None

        def poolturn_at(i):
            return (i - 4) // 2 if i in (4, 6, 8, 10) else None

        def keys_at(i):
            return i - 20 if 20 <= i < 24 else None

        turn_plan, turn_step = [], []
        for i in range(ITEMS + 1):
            if is_turned(i - 1):
                turn_plan.append((item(i - 1)[0], item(i - 1)[1]))
            if poolturn_at(i) is not None:
                turn_plan.append(("pool", poolturn_at(i)))
            if keys_at(i) is not None:
                turn_plan.append(("keys", keys_at(i)))
            turn_step += [i] * (len(turn_plan) - len(turn_step))

        def turns_before(i):
            n = len([m for m in range(i - 1) if is_turned(m)])
            items = [t for t, (ch, _) in enumerate(turn_plan) if ch in (1, 2, 4, 5)]
            return TURN_X + items[n - 1] + 1

        stage_plan = [("q", j) if ch == 1 else ("qi", j) if ch == 4 else ("pool", j)
                      for ch, j in turn_plan if ch in (1, 4, "pool")]
        SLAB = {"q": 0, "qi": 1, "pool": 2}
        TURNS = TURN_X + len(turn_plan)

        def keys_of(j):
            return (j + 1) * P

        behind = {}
        for j in range(NT):
            for n in range(SPLIT if j == 0 else 0, PIECES):
                s_at = SLOTS * j - 3 + SLOTS * (sum(WEIGHT[:n]) - sum(WEIGHT[:SPLIT])) // sum(WEIGHT)
                behind.setdefault(max(s_at, 0), []).append((j, n))

        block = ctx.enter_context(nc.Block())

        @block.sync
        def _(sp):
            rows = [(R_C, c.rearrange("a (r n) -> (a r) n", n=P), 8),
                    (R_ADAB, ada_b.rearrange("a (r n) -> (a r) n", n=P), 48),
                    (R_N1, norm1_g.rearrange("a (r n) -> (a r) n", n=P), 8),
                    (R_N2, norm2_g.rearrange("a (r n) -> (a r) n", n=P), 8),
                    (R_OG, pool_out_g.rearrange("a (r n) -> (a r) n", n=P), 4),
                    (R_OG + 4, attn_out_g.rearrange("a (r b) n -> (a r) (b n)", b=2), 4)]
            for at, src, n in rows:
                sp.dma_start(prm[at:at + n, :], src).then_inc(rows_in, 16)
            for half in range(2):
                for at, g in ((R_QG, q_norm_g), (R_KG, k_norm_g)):
                    sp.dma_start(prm[at:at + 1, half * HD:half * HD + HD], g).then_inc(rows_in, 16)
            sp.dma_start(cst[:, :], const[:, 0:NCST]).then_inc(cst_in, 16)
            for j in range(NT):
                sp.dma_start(x_all[:, j, :], x[0, j * P:(j + 1) * P, :]).then_inc(x_in[j], 16)

            def load_chunk(n):
                kind, m, b = stream[n]
                before = in_buffer[b][:at_stream[kind, m][1] - 1]
                if before:
                    was, o = before[-1]
                    sp.wait_ge(*((partial_ready[o % 2], o // 2 + 1) if was == "ada" else (projected, NT * (o + 1))))
                if kind == "ada":
                    src, w = ada_w[0, :, m * 512:(m + 1) * 512], 512
                else:
                    ch = IN_ORDER[m]
                    src, w = w_in[0, :, ch * 512:ch * 512 + width(ch)], width(ch)
                sp.dma_start(chunks[b][:, :, 0:w],
                             src.rearrange("(k p) n -> p k n", p=P)).then_inc(chunk_in[b], 16)

            for n in range(3):
                load_chunk(n)
            load_chunk(3)
            sp.dma_start(bands, const[:, NCST:].rearrange("p (b n) -> p b n", b=12)).then_inc(pool_in, 16)
            sp.dma_start(poolw, pool_w[0].rearrange("g c d -> c g d")).then_inc(pool_in, 16)
            sp.dma_start(pscale, pool_scale[0:1, :].broadcast_to([P, 512])).then_inc(pool_in, 16)
            for n in range(4, 8):
                load_chunk(n)
            sp.dma_start(wout_sb[:, :, :], w_out[0].rearrange("(k p) n -> p k n", p=P)).then_inc(wout_in, 16)
            sp.wait_ge(turned, TURN_X)
            sp.dma_start(sk_raw, peer_subkeys[0].rearrange("h s n d -> n (h s) d")).then_inc(sk_in, 16)
            for n in range(8, len(stream)):
                load_chunk(n)

            def load_queries(j):
                if j == 0:
                    for b in range(3):
                        sp.wait_ge(spilled[b], 16 * len(stage_plan[b::3]))
                else:
                    sp.wait_ge(out_proj, j)
                sp.dma_start(tile_in[:, :, :], spill[j].rearrange("a p n -> p a n")).then_inc(tile_loaded, 16)

            def load_x(j):
                if j == 0:
                    sp.wait_ge(projected, ITEMS)
                else:
                    sp.wait_ge(x2_saved, 16 * j)
                    sp.wait_ge(xn2_ready, j)
                    sp.wait_ge(x2_squared, j)
                sp.dma_start(xt, x[0, j * P:(j + 1) * P, :]).then_inc(xt_loaded, 16)

            wq_v = peer_wq[0].rearrange("(k p) n -> p k n", p=P)

            def load_wq(g):
                sp.dma_start(wq_sb[:, g, :, :], wq_v[:, :, g * 512:(g + 1) * 512]).then_inc(wq_in[g], 16)

            sp.wait_ge(mixed, NT)
            load_wq(2)
            load_queries(0)
            sp.wait_ge(modcol_ready, 12)
            load_wq(3)
            sp.wait_ge(turned, TURNS)
            load_wq(0)
            load_x(0)
            load_wq(1)

            def finish_tile(j):
                if j >= 1:
                    sp.wait_ge(out_saved, 16 * j)
                sp.dma_start(fin[:, :], x2_dram[j * P:(j + 1) * P, :]).then_inc(fin_loaded, 16)

            for j in range(NT):
                sp.wait_ge(x2_ready, j + 1)
                sp.dma_start(x2_dram[j * P:(j + 1) * P, :], xt).then_inc(x2_saved, 16)
                if j + 1 < NT:
                    load_queries(j + 1)
                    load_x(j + 1)
                if j >= 1:
                    sp.wait_ge(fin_ready, j)
                    sp.dma_start(out[0, (j - 1) * P:j * P, :], fin[:, :]).then_inc(out_saved, 16)
                if j == 0:
                    sp.wait_ge(x2_saved, 16)
                else:
                    sp.wait_ge(x2_saved, 16 * (j + 1))
                finish_tile(j)
            sp.wait_ge(fin_ready, NT)
            sp.dma_start(out[0, (NT - 1) * P:, :], fin[:, :]).then_inc(out_saved, 16)
            sp.wait_ge(out_saved, 16 * NT)

        @block.gpsimd
        def _(pool):
            steps = 0
            pool.wait_ge(scol_ready, 1)
            for a in BY_POOL:
                w = chunk_loaded(pool, "ada", a)
                if a >= 2:
                    pool.wait_ge(modcol_ready, a - 1)
                nc.gpsimd.tensor_tensor(w, w, scol.unsqueeze(2).broadcast_to([P, KT, 512]), ALU.mult).then_inc(pool_step, 1)
                for half in (4, 2, 1):
                    steps += 1
                    pool.wait_ge(pool_step, steps)
                    o = w[:, 0:half, :] if half > 1 else partial[:, a % 2:a % 2 + 1, :]
                    nc.gpsimd.tensor_tensor(o, w[:, 0:half, :], w[:, half:2 * half, :], ALU.add).then_inc(
                        pool_step if half > 1 else partial_ready[a % 2], 1)

            def gather(table, buf, landed, used, s):
                if s >= NB:
                    pool.wait_ge(used, s - NB + 1)
                    pool.wait_ge(landed[s % NB], 16 * (s // NB))
                j, r = divmod(s, SLOTS)
                pool.indirect_dma_start(
                    buf[s % NB], None, table,
                    bass.IndirectOffsetOnAxis(ap=eid[:, j % 2, r:r + 1], axis=0),
                ).then_inc(landed[s % NB], 16)

            pool.wait_ge(projected, ITEMS)
            for s in range(NT * SLOTS + PK):
                if s < NT * SLOTS:
                    if s % (2 * PK) == 0:
                        pool.wait_ge(experts_ready, s // (2 * PK) + 1)
                    gather(peer_u[0], ubuf, u_landed, u_used, s)
                if s >= PK:
                    gather(peer_v[0], vbuf, v_landed, v_used, s - PK)

        @block.tensor
        def _(pe):
            mm = nc.tensor.matmul
            pe.wait_ge(rows_in, 16 * 10)
            pe.wait_ge(cst_in, 16)
            nc.tensor.transpose(acc[1][:, 0:NROWS], prm[0:NROWS, :], ident[0:NROWS, 0:NROWS]).then_inc(rowsT_ready, 1)

            def ada_cols(a):
                partial_made(pe, a)
                for b in range(4):
                    last = mm(modcol[:, 4 * a + b:4 * a + b + 1], partial[:, a % 2, b * P:(b + 1) * P], ones[:, :],
                              start=True, stop=True)
                last.then_inc(modcol_ready, 1)

            pe.wait_ge(cols_ready, 1)
            for a in range(4):
                ada_cols(a)

            def turn_bank(n, src, blocks=4):
                if n >= 2:
                    pe.wait_ge(turn_taken, n - 1)
                for b in range(blocks):
                    last = nc.tensor.transpose(T[n % 2][:, b * P:(b + 1) * P], src[:, b * P:(b + 1) * P], ident)
                last.then_inc(turned, 1)

            def turn_x(j):
                pe.wait_ge(xn_ready, j + 1)
                for half in range(2):
                    turn_bank(2 * j + half, x_all[:, j, half * 512:(half + 1) * 512])

            turn_x(0)
            turn_x(1)
            turns = TURN_X
            for i in range(ITEMS + 1):
                if i < ITEMS:
                    ch, j = item(i)
                    w = chunk_loaded(pe, "in", i // NT)
                    pe.wait_ge(turn_taken, 2 * j + 2)
                    if i >= 2:
                        item_left(pe, i - 2)
                    for k in range(KT):
                        last = mm(A[i % 2][:, 0:width(ch)], hT[:, k, j * P:(j + 1) * P], w[:, k, 0:width(ch)],
                                  start=(k == 0), stop=(k == KT - 1))
                    last.then_inc(projected, 1)
                if i + 2 < NT:
                    turn_x(i + 2)
                if i - 1 in ADA_AT:
                    ada_cols(ADA_AT[i - 1])
                if is_turned(i - 1):
                    pe.wait_ge(normed_ready[(i - 1) % 2], normed_count(i - 1))
                    turn_bank(turns, normed[:, (i - 1) % 2, :], 1 if item(i - 1)[0] == 5 else 4)
                    turns += 1
                if (j := pooled_at(i)) is not None:
                    pe.wait_ge(pool_in, 48)
                    pe.wait_ge(item_taken[j % 2], j // 2 + 1)
                    if j >= 1:
                        pe.wait_ge(pooled_taken, j)
                    for g in range(4):
                        o = B[0][:, g * P:(g + 1) * P]
                        last = mm(o, u_all[:, j, g * P:(g + 1) * P], bands[:, g if j == 0 else 4 + g, :],
                                  start=True, stop=(j == 0))
                        if j >= 1:
                            last = mm(o, u_all[:, j - 1, g * P:(g + 1) * P], bands[:, 8 + g, :], start=False, stop=True)
                    last.then_inc(pooled, 1)
                if (j := mix_at(i)) is not None:
                    pe.wait_ge(pooled_taken, j + 1)
                    pe.wait_ge(poolw_ready, 1)
                    if j >= 1:
                        pe.wait_ge(mixed_taken, j)
                    for g in range(4):
                        last = mm(B[1][:, g * P:(g + 1) * P], pooled_sb[:, g * P:(g + 1) * P],
                                  poolw[:, g * P:(g + 1) * P], start=True, stop=True)
                    last.then_inc(mixed, 1)
                if (j := poolturn_at(i)) is not None:
                    pe.wait_ge(mixed_taken, j + 1)
                    turn_bank(turns, pool_n)
                    turns += 1
                if keys_at(i) is not None:
                    g = keys_at(i)
                    pe.wait_ge(sk_in, 16)
                    turn_bank(turns, sk_raw[:, 4 * g:4 * g + 4, :].rearrange("p b n -> p (b n)"))
                    turns += 1
                if ROW_AT <= i < ROW_AT + 4:
                    r = i - ROW_AT
                    pe.wait_ge(mod_taken, 1)
                    if r >= 1:
                        pe.wait_ge(row_taken, r)
                    col = (g1c, g2c)[r // 2]
                    for b in range(4):
                        k = 4 * (r % 2) + b
                        last = mm(acc[0][:, b * P:(b + 1) * P], col[:, k:k + 1].broadcast_to([P, P]), ident,
                                  start=True, stop=True)
                    last.then_inc(row_ready, 1)

            def front_piece(j, i):
                W = keys_of(j)
                qT, qiT, plT = (tile_in[:, n, :] for n in range(3))
                if i < TOP:
                    if j == 0 or i >= 8:
                        return
                    if i == 0:
                        pe.wait_ge(tile_loaded, 16 * (j + 1))
                        pe.wait_ge(pscores_taken, 4 * j)
                    if i >= 2:
                        pe.wait_ge(relu_done, 8 * (j - 1) + i - 1)
                    o = HD * (i % 2)
                    mm(A[i % 2][:, 0:W], qiT[o:o + HD, (i // 2) * P:(i // 2 + 1) * P], kidxT[o:o + HD, 0:W],
                       start=True, stop=True).then_inc(dotted, 1)
                elif ATT <= i < END:
                    h = i - ATT
                    if h < HEADS:
                        if h == 0:
                            if j == 0:
                                item_left(pe, ITEMS - 2)
                                item_left(pe, ITEMS - 1)
                                pe.wait_ge(tile_loaded, 16)
                            else:
                                pe.wait_ge(relu_done, 8 * j)
                        if h >= 2:
                            pe.wait_ge(biased, 8 * j + h - 1)
                        o = HD * (h % 2)
                        mm(A[h % 2][:, 0:W], qT[o:o + HD, (h // 2) * P:(h // 2 + 1) * P], keysT[o:o + HD, h // 2, 0:W],
                           start=True, stop=True).then_inc(logits, 1)
                    if 1 <= h <= HEADS:
                        h -= 1
                        pe.wait_ge(expd, 8 * j + h + 1)
                        if h < 2:
                            pe.wait_ge(turn_taken, TURNS)
                            if j >= 1:
                                pe.wait_ge(h2_ready, 2 * j)
                        else:
                            pe.wait_ge(probT_taken, 8 * j + h - 1)
                        for b in range(j + 1):
                            last = nc.tensor.transpose(T[h % 2][:, b * P:(b + 1) * P], pr[:, h % 2, b * P:(b + 1) * P], ident)
                        last.then_inc(probT, 1)
                        h += 1
                    if h >= 2:
                        h -= 2
                        pe.wait_ge(probT_taken, 8 * j + h + 1)
                        if h == 0 and j >= 1:
                            pe.wait_ge(att_read, j)
                        for b in range(j + 1):
                            last = mm(B[0][:, h * HD:(h + 1) * HD], prT[:, h % 2, b * P:(b + 1) * P],
                                      vals[:, b, h * HD:(h + 1) * HD], start=(b == 0), stop=(b == j))
                        last.then_inc(pv_done, 1)
                elif i == ATT_TURN:
                    pe.wait_ge(att_ready, j + 1)
                    pe.wait_ge(probT_taken, 8 * j + 8)
                    for b in range(4):
                        last = nc.tensor.transpose(T[0][:, b * P:(b + 1) * P], score[:, b * P:(b + 1) * P], ident)
                    last.then_inc(attT_ready, 1)
                elif OUT_PROJ <= i < X2:
                    part = i - OUT_PROJ
                    if part == 0:
                        pe.wait_ge(biased, 8 * j + 8)
                        pe.wait_ge(row_taken, 2)
                    if part == 2:
                        pe.wait_ge(attT_taken, j + 1)
                    for k in (2 * part, 2 * part + 1):
                        src = plT[:, k * P:(k + 1) * P] if k < 4 else attT[:, (k - 4) * P:(k - 3) * P]
                        for half in range(2):
                            last = mm(A[half][:, :], src, wout_sb[:, k, half * 512:(half + 1) * 512],
                                      start=(k == 0), stop=(k == KT - 1))
                    if part == 3:
                        last.then_inc(out_proj, 1)
                elif i == H2T:
                    pe.wait_ge(xn2_ready, j + 1)
                    for b in range(KT):
                        last = nc.tensor.transpose(T[b // 4][:, (b % 4) * P:(b % 4 + 1) * P],
                                                   front[:, 1 + j % 2, b * P:(b + 1) * P], ident)
                        if b % 4 == 3:
                            last.then_inc(xn2T, 1)
                elif i == H2:
                    for half in range(2):
                        pe.wait_ge(h2T_ready, 2 * j + half + 1)
                        for b in range(4):
                            k = 4 * half + b
                            last = nc.tensor.transpose(T[half][:, b * P:(b + 1) * P], h2T[:, k * P:(k + 1) * P], ident)
                        last.then_inc(h2_turned, 1)
                elif i >= PEER:
                    g, b = divmod(i - PEER, 4)
                    if b == 0 and 1 <= g <= 4:
                        n = 4 * j + g - 1
                        pe.wait_ge(pq_taken, n + 1)
                        if g - 1 < 2:
                            pe.wait_ge(x2_ready, j + 1)
                        else:
                            pe.wait_ge(pscores_taken, n - 1)
                        for m in range(4):
                            last = mm(A[(g - 1) % 2][:, m * P:(m + 1) * P], prT[:, 0, m * P:(m + 1) * P],
                                      skT[:, 4 * (g - 1) + m, :], start=True, stop=True)
                        last.then_inc(pscores, 1)
                    if g < 4:
                        if b == 0:
                            pe.wait_ge(wq_in[g], 16)
                            pe.wait_ge(h2T_ready, 2 * j + 2)
                            if 4 * j + g >= 1:
                                pe.wait_ge(pq_taken, 4 * j + g)
                        for k in range(KT):
                            last = mm(B[1][:, b * P:(b + 1) * P], wq_sb[:, g, k, b * P:(b + 1) * P],
                                      h2T[:, k * P:(k + 1) * P], start=(k == 0), stop=(k == KT - 1))
                        if b == 3:
                            last.then_inc(pq_done, 1)

            for i in range(SPLIT):
                front_piece(0, i)
            for s in range(NT * SLOTS + PK):
                m = s - PK
                if m >= 0:
                    j, r = divmod(m, SLOTS)
                    if r == 0 and j == 0:
                        pe.wait_ge(row_taken, 4)
                    if r == 0 and j >= 1:
                        pe.wait_ge(fin_ready, j)
                    pe.wait_ge(diag_ready, m + 1)
                    pe.wait_ge(v_landed[m % NB], 16 * (m // NB + 1))
                    for half in range(2):
                        last = mm(acc[half][:, :], diag[:, m % NB, :], vbuf[m % NB][:, half * 512:(half + 1) * 512],
                                  start=(r == 0), stop=(r == SLOTS - 1))
                    last.then_inc(v_used, 1)
                for piece in behind.get(s, ()):
                    front_piece(*piece)

        @block.scalar
        def _(act):
            steps = [0]

            def link(ins):
                steps[0] += 1
                ins.then_inc(act_step, 1)
                act.wait_ge(act_step, steps[0])

            fn = nc.scalar.activation
            act.wait_ge(cols_ready, 1)
            fn(ecol, cols[:, R_C:R_C + 8], ACT.Exp, scale=-1.0).then_inc(exp_c, 1)
            for j in range(NT):
                act.wait_ge(x_in[j], 16)
                if j >= 2:
                    act.wait_ge(xss_ready, j - 1)
                fn(u_all[:, 2 * (j % 2):2 * (j % 2) + 2, :].rearrange("p a n -> p (a n)"), x_all[:, j, :], ACT.Square,
                   accum_out=ssx[:, j:j + 1]).then_inc(xss_ready, 1)
            act.wait_ge(xss_ready, NT)

            staged_at = [t for t, (ch, _) in enumerate(turn_plan) if ch in (1, 4, "pool")]

            def save_staged(step):
                for e, t in enumerate(staged_at):
                    if turn_step[t] == step:
                        what, j = stage_plan[e]
                        act.wait_ge(turn_taken, TURN_X + t + 1)
                        act.dma_start(spill[j, SLAB[what]], stage[:, e % 3, :]).then_inc(spilled[e % 3], 16)

            for i in range(ITEMS):
                ch, j = item(i)
                act.wait_ge(projected, i + 1)
                src = A[i % 2][:, 0:512]
                if ch == 0:
                    fn(u_all[:, j, :], src, ACT.Copy).then_inc(item_taken[i % 2], 1)
                elif ch in (1, 2):
                    if normed_count(i) > 1:
                        act.wait_ge(normed_ready[i % 2], normed_count(i) - 1)
                    fn(square[:, i % 2, :], src, ACT.Square).then_inc(item_squared, 1)
                elif ch == 3:
                    fn(vals[:, j, :], src, ACT.Copy).then_inc(item_taken[i % 2], 1)
                elif ch == 4:
                    act.wait_ge(turned, turns_before(i))
                    act.wait_ge(normed_ready[i % 2], normed_count(i) - 1)
                    fn(normed[:, i % 2, :], src, ACT.Copy).then_inc(normed_ready[i % 2], 1)
                if (t := pooled_at(i)) is not None:
                    act.wait_ge(pooled, t + 1)
                    if t >= 1:
                        act.wait_ge(mixed_taken, t)
                    fn(pooled_sb, B[0][:, :], ACT.Copy).then_inc(pooled_taken, 1)
                if (t := mix_at(i)) is not None:
                    act.wait_ge(mixed, t + 1)
                    fn(pooled_sb, B[1][:, :], ACT.Square, accum_out=sspool[:, t:t + 1]).then_inc(mixed_squared, 1)
                save_staged(i - 1)

            def front_piece(j, i):
                W = keys_of(j)
                if i < TOP:
                    if j == 0 or i >= 8:
                        return
                    n = 8 * (j - 1) + i
                    act.wait_ge(dotted, n + 1)
                    if i >= 2:
                        act.wait_ge(relu_used, n - 1)
                    else:
                        act.wait_ge(probT, 8 * j)
                        if n >= 2:
                            act.wait_ge(relu_used, n - 1)
                    fn(pr[:, i % 2, 0:W], A[i % 2][:, 0:W], ACT.Relu).then_inc(relu_done, 1)
                elif ATT <= i < END:
                    h = i - ATT
                    if h < HEADS:
                        n = 8 * j + h
                        act.wait_ge(biased, n + 1)
                        if n >= 2:
                            act.wait_ge(probT, n - 1)
                        if h < 2 and j >= 1:
                            act.wait_ge(relu_used, 8 * j)
                        fn(pr[:, h % 2, 0:W], lg[:, h % 2, 0:W], ACT.Exp, bias=mn8[:, h:h + 1], scale=-1.0,
                           accum_out=rs8[:, h:h + 1]).then_inc(expd, 1)
                    if 1 <= h <= HEADS:
                        n = 8 * j + h - 1
                        act.wait_ge(probT, n + 1)
                        if h - 1 < 2 and j >= 1:
                            act.wait_ge(pscores, 4 * j)
                        if n >= 2:
                            act.wait_ge(pv_done, n - 1)
                        fn(prT[:, (h - 1) % 2, 0:W], T[(h - 1) % 2][:, 0:W], ACT.Copy).then_inc(probT_taken, 1)
                elif i == ATT_TURN:
                    act.wait_ge(attT_ready, j + 1)
                    if j >= 1:
                        act.wait_ge(out_proj, j)
                    fn(attT[:, :], T[0][:, :], ACT.Copy).then_inc(attT_taken, 1)
                elif i == X2:
                    act.wait_ge(x2_ready, j + 1)
                    if j >= 1:
                        act.wait_ge(pq_done, 4 * j)
                    fn(h2T, xt, ACT.Square, accum_out=ssx[:, 0:1]).then_inc(x2_squared, 1)
                elif i == H2:
                    for half in range(2):
                        act.wait_ge(h2_turned, 2 * j + half + 1)
                        fn(front[:, 1 + j % 2, half * 512:(half + 1) * 512], T[half][:, :], ACT.Copy).then_inc(h2_ready, 1)
                elif i >= PEER:
                    g, b = divmod(i - PEER, 4)
                    if b == 3 and g < 4:
                        act.wait_ge(pq_done, 4 * j + g + 1)
                        if g == 0:
                            act.wait_ge(pv_done, 8 * j + 8)
                        else:
                            act.wait_ge(pscores, 4 * j + g)
                        fn(prT[:, 0, :], B[1][:, :], ACT.Copy).then_inc(pq_taken, 1)
                    if b == 3 and g >= 1:
                        act.wait_ge(gate_in, 4 * j + g)
                        g2 = gates[:, j % 2, 32 * (g - 1):32 * g]
                        fn(g2, g2, ACT.Exp).then_inc(gate_exp, 1)

            for i in range(SPLIT):
                front_piece(0, i)
            for s in range(NT * SLOTS + PK):
                m = s - PK
                n, k = divmod(s, PK)
                if k == 0 and n >= 1:
                    act.wait_ge(u_used, PK * n)
                    if n >= 3:
                        act.wait_ge(wts_ready, n - 2)
                    fn(gel[:, (n - 1) % 2, :], dots[:, (n - 1) % 2, :], ACT.Gelu).then_inc(gelu_done, 1)
                if m >= 0:
                    q = m // PK
                    act.wait_ge(wts_ready, q + 1)
                    if m >= NB:
                        act.wait_ge(v_used, m - NB + 1)
                    fn(diag[:, m % NB, :], ident, ACT.Copy, scale=wts[:, q % 2, k:k + 1]).then_inc(diag_ready, 1)
                for piece in behind.get(s, ()):
                    front_piece(*piece)

        @block.vector
        def _(dve):
            steps, newest = [0], []
            v = nc.vector

            def step(ins):
                steps[0] += 1
                return tell(ins, dve_step, steps[0])

            def tell(ins, s, value):
                ins.then_inc(s, 1)
                newest[:] = [(s, value)]
                return s, value

            def after(mark=None):
                dve.wait_ge(*(mark or newest[0]))
                return v

            def rsqrt(y, var, t):
                step(after().tensor_scalar(t.bitcast(U32), var.bitcast(U32), 1, None, ALU.logical_shift_right))
                step(after().tensor_scalar(y.bitcast(U32), t.bitcast(U32), -1.0, float(0x5F3759DF), ALU.mult, ALU.add))
                for _ in range(3):
                    step(after().tensor_tensor(t, y, y, ALU.mult))
                    step(after().scalar_tensor_tensor(out=t, in0=t, scalar=-0.5, in1=var, op0=ALU.mult, op1=ALU.mult))
                    step(after().scalar_tensor_tensor(out=y, in0=t, scalar=1.5, in1=y, op0=ALU.add, op1=ALU.mult))

            step(v.memset(ones[:, :], 1.0))
            dve.wait_ge(rowsT_ready, 1)
            tell(v.tensor_copy(cols[:, 0:NROWS], acc[1][:, 0:NROWS]), cols_ready, 1)
            dve.wait_ge(exp_c, 1)
            step(after().tensor_scalar(ecol, ecol, 1.0, None, ALU.add))
            step(after().reciprocal(ecol, ecol))
            tell(after().tensor_tensor(scol, ecol, cols[:, R_C:R_C + 8], ALU.mult), scol_ready, 1)

            dve.wait_ge(xss_ready, NT)
            step(v.tensor_scalar(var8[:, 0:NT], ssx, 1.0 / D, EPS, ALU.mult, ALU.add))
            rsqrt(y8[:, 0:NT], var8[:, 0:NT], t8[:, 0:NT])
            after()
            for j in range(NT):
                v.tensor_scalar(x_all[:, j, :], x_all[:, j, :], y8[:, j:j + 1], None, ALU.mult).then_inc(xn_ready, 1)

            def ada_partial(a):
                w, marks = chunk_loaded(dve, "ada", a), [newest[0], newest[0]]
                if a >= 2:
                    dve.wait_ge(modcol_ready, a - 1)
                for k in range(KT):
                    for half in range(2):
                        cut = slice(256 * half, 256 * half + 256)
                        o = partial[:, a % 2, cut]
                        after(marks[half])
                        if k == 0:
                            ins = v.tensor_scalar(o, w[:, 0, cut], scol[:, 0:1], None, ALU.mult)
                        else:
                            ins = v.scalar_tensor_tensor(out=o, in0=w[:, k, cut], scalar=scol[:, k:k + 1], in1=o,
                                                         op0=ALU.mult, op1=ALU.add)
                        if (k, half) == (KT - 1, 1):
                            tell(ins, partial_ready[a % 2], a // 2 + 1)
                        else:
                            marks[half] = step(ins)

            dve.wait_ge(scol_ready, 1)
            step(v.memset(small[:, 96:97], 0.0))
            for a in (0, 2, 3):
                ada_partial(a)
            dve.wait_ge(modcol_ready, 4)
            step(v.tensor_tensor(b1, modcol[:, 0:8], cols[:, R_ADAB:R_ADAB + 8], ALU.add))
            step(v.tensor_tensor(a1, modcol[:, 8:16], cols[:, R_ADAB + 8:R_ADAB + 16], ALU.add))
            step(after().scalar_tensor_tensor(out=a1, in0=a1, scalar=1.0, in1=cols[:, R_N1:R_N1 + 8], op0=ALU.add, op1=ALU.mult))
            after()
            turns = 0
            for j in range(NT):
                for half in range(2):
                    dve.wait_ge(turned, turns + 1)
                    for b in range(4):
                        k = 4 * half + b
                        last = v.tensor_scalar(hT[:, k, j * P:(j + 1) * P], T[turns % 2][:, b * P:(b + 1) * P],
                                               a1[:, k:k + 1], b1[:, k:k + 1], ALU.mult, ALU.add)
                    turns += 1
                    tell(last, turn_taken, turns)
            dve.wait_ge(pool_in, 48)
            tell(v.tensor_tensor(poolw, poolw, pscale, ALU.mult), poolw_ready, 1)

            staged = 0

            def take_turn(what, j):
                nonlocal turns, staged
                dve.wait_ge(turned, turns + 1)
                src = T[turns % 2]
                turns += 1
                if what == 2:
                    last = v.tensor_scalar(keysT[:, :, j * P:(j + 1) * P], src[:, :].rearrange("p (a n) -> p a n", a=4),
                                           cols[:, R_KG:R_KG + 1], None, ALU.mult)
                elif what == 5:
                    last = v.tensor_copy(kidxT[:, j * P:(j + 1) * P], src[:, 0:P])
                elif what == "keys":
                    last = v.tensor_copy(skT[:, 4 * j:4 * j + 4, :].rearrange("p a n -> p (a n)"), src[:, :])
                else:
                    e = staged
                    staged += 1
                    if e >= 3:
                        dve.wait_ge(spilled[e % 3], 16 * (e // 3))
                    if what == 1:
                        last = v.tensor_scalar(stage[:, e % 3, :], src[:, :], cols[:, R_QG:R_QG + 1], None, ALU.mult)
                    else:
                        last = v.tensor_copy(stage[:, e % 3, :], src[:, :])
                tell(last, turn_taken, turns)

            for i in range(ITEMS + 1):
                if i < ITEMS:
                    ch, j = item(i)
                    b = i % 2
                    n3 = normed[:, b, :].rearrange("p (h n) -> p h n", h=8)
                    if ch in (1, 2):
                        dve.wait_ge(item_squared, sum(1 for m in range(i + 1) if item(m)[0] in (1, 2)))
                        step(after().reduce_sum(ss8, square[:, b, :].rearrange("p (h n) -> p h n", h=8), AX_X))
                        step(after().tensor_scalar(var8, ss8, 1.0 / HD, EPS, ALU.mult, ALU.add))
                        rsqrt(y8, var8, t8)
                        step(after().tensor_tensor(y8, y8, cst[:, C_HK + 8 * (ch - 1):C_HK + 8 * ch], ALU.mult))
                        dve.wait_ge(turned, turns)
                        tell(after().tensor_tensor(n3, A[b][:, :].rearrange("p (h n) -> p h n", h=8),
                                                   y8.unsqueeze(2).broadcast_to([P, 8, HD]), ALU.mult),
                             normed_ready[b], normed_count(i))
                    elif ch == 5:
                        dve.wait_ge(projected, i + 1)
                        dve.wait_ge(turned, turns)
                        dve.wait_ge(normed_ready[b], normed_count(i) - 1)
                        v.tensor_scalar(widx[:, j, :], A[b][:, HD:HD + 8], float(np.float32(8 ** -0.5)),
                                        HD ** -0.5, ALU.mult, ALU.mult)
                        v.tensor_copy(normed[:, b, 0:HD], A[b][:, 0:HD])
                        tell(v.tensor_copy(normed[:, b, HD:P], A[b][:, 0:HD]), normed_ready[b], normed_count(i))
                if is_turned(i - 1):
                    take_turn(*item(i - 1))
                if (j := mix_at(i)) is not None:
                    dve.wait_ge(mixed_squared, j + 1)
                    step(after().tensor_scalar(var8[:, 0:1], sspool[:, j:j + 1], 1.0 / 512, EPS, ALU.mult, ALU.add))
                    rsqrt(y8[:, 0:1], var8[:, 0:1], t8[:, 0:1])
                    dve.wait_ge(turned, turns)
                    tell(after().tensor_scalar(pool_n, B[1][:, :], y8[:, 0:1], None, ALU.mult), mixed_taken, j + 1)
                if (j := poolturn_at(i)) is not None:
                    take_turn("pool", j)
                if keys_at(i) is not None:
                    take_turn("keys", keys_at(i))
                if i in DVE_ADA_AT:
                    ada_partial(DVE_ADA_AT[i])
                if i == MODS_AT:
                    dve.wait_ge(modcol_ready, 12)
                    ab = cols[:, R_ADAB:R_ADAB + 48]
                    v.tensor_tensor(g1c, modcol[:, 16:24], ab[:, 16:24], ALU.add)
                    v.tensor_tensor(g2c, modcol[:, 40:48], ab[:, 40:48], ALU.add)
                    v.tensor_tensor(b2, modcol[:, 24:32], ab[:, 24:32], ALU.add)
                    step(v.tensor_tensor(a2, modcol[:, 32:40], ab[:, 32:40], ALU.add))
                    tell(after().scalar_tensor_tensor(out=a2, in0=a2, scalar=1.0, in1=cols[:, R_N2:R_N2 + 8],
                                                      op0=ALU.add, op1=ALU.mult), mod_taken, 1)
                if ROW_AT <= i < ROW_AT + 4:
                    r = i - ROW_AT
                    half = slice(512 * (r % 2), 512 * (r % 2) + 512)
                    dve.wait_ge(row_ready, r + 1)
                    if r < 2:
                        dve.wait_ge(wout_in, 16)
                        for k in range(KT):
                            w = wout_sb[:, k, half]
                            last = v.scalar_tensor_tensor(out=w, in0=w, scalar=cols[:, R_OG + k:R_OG + k + 1],
                                                          in1=acc[0][:, :], op0=ALU.mult, op1=ALU.mult)
                    else:
                        last = v.tensor_copy(gate2[:, half], acc[0][:, :])
                    tell(last, row_taken, r + 1)

            def front_piece(j, i):
                W = keys_of(j)
                dist = cst[:, C_DIST + SEQ - W:C_DIST + SEQ]
                if i < TOP:
                    i -= 1
                    if j == 0 or i < 0:
                        return
                    n = 8 * (j - 1) + i
                    if i == 0:
                        dve.wait_ge(attT_ready, j)
                    else:
                        dve.wait_ge(relu_used, n)
                    dve.wait_ge(relu_done, n + 1)
                    w = widx[:, j, i:i + 1]
                    if i == 0:
                        ins = after().tensor_scalar(score[:, 0:W], pr[:, 0, 0:W], w, None, ALU.mult)
                    else:
                        ins = v.scalar_tensor_tensor(out=score[:, 0:W], in0=pr[:, i % 2, 0:W], scalar=w,
                                                     in1=score[:, 0:W], op0=ALU.mult, op1=ALU.add)
                    tell(ins, relu_used, n + 1)
                elif i < ATT:
                    if j == 0:
                        if i == TOP:
                            step(after().tensor_copy(bias[:, 0:W], dist))
                            step(after().memset(bias[0:HD, W - HD:W], MASKED))
                        return
                    if i == TOP:
                        step(after().memset(score[0:HD, W - HD:W], -MASKED))
                    if i < TOP + TOPK // 8:
                        step(after().max(m8, score[:, 0:W]))
                        step(after().match_replace(out=score[:, 0:W], in_to_replace=m8, in_values=score[:, 0:W],
                                                   imm_value=TAKEN))
                    else:
                        step(after().tensor_scalar(score[:, 0:W], score[:, 0:W], -2e38, MASKED, ALU.is_gt, ALU.mult))
                        step(after().tensor_tensor(bias[:, 0:W], score[:, 0:W], dist, ALU.add))
                elif i < END:
                    h = i - ATT
                    if h < HEADS:
                        n = 8 * j + h
                        dve.wait_ge(logits, n + 1)
                        if n >= 2:
                            dve.wait_ge(expd, n - 1 if h else 8 * j)
                        tell(after().tensor_tensor_reduce(
                            out=lg[:, h % 2, 0:W], in0=bias[:, 0:W], in1=A[h % 2][:, 0:W], scale=2.0 ** -(h + 1),
                            scalar=3e38, op0=ALU.add, op1=ALU.min, accum_out=mn8[:, h:h + 1]), biased, n + 1)
                elif i == END:
                    dve.wait_ge(pv_done, 8 * j + 8)
                    o3 = score[:, :].rearrange("p (h n) -> p h n", h=8)
                    sq = lg[:, 0, :]
                    step(after().reciprocal(rr8, rs8))
                    tell(after().tensor_tensor(o3, B[0][:, :].rearrange("p (h n) -> p h n", h=8),
                                               rr8.unsqueeze(2).broadcast_to([P, 8, HD]), ALU.mult), att_read, j + 1)
                    step(after().tensor_tensor(sq, score[:, :], score[:, :], ALU.mult))
                    step(after().reduce_sum(ss8, sq.rearrange("p (h n) -> p h n", h=8), AX_X))
                    step(after().tensor_scalar(var8, ss8, 1.0 / HD, EPS, ALU.mult, ALU.add))
                    rsqrt(y8, var8, t8)
                    tell(after().tensor_tensor(o3, o3, y8.unsqueeze(2).broadcast_to([P, 8, HD]), ALU.mult),
                         att_ready, j + 1)
                elif i == X2:
                    dve.wait_ge(xt_loaded, 16 * (j + 1))
                    dve.wait_ge(out_proj, j + 1)
                    v.tensor_tensor(xt[:, 0:512], xt[:, 0:512], A[0][:, :], ALU.add)
                    tell(v.tensor_tensor(xt[:, 512:1024], xt[:, 512:1024], A[1][:, :], ALU.add), x2_ready, j + 1)
                elif i == XN2:
                    dve.wait_ge(x2_squared, j + 1)
                    step(after().tensor_scalar(var8[:, 0:1], ssx[:, 0:1], 1.0 / D, EPS, ALU.mult, ALU.add))
                    rsqrt(y8[:, 0:1], var8[:, 0:1], t8[:, 0:1])
                    if j >= 2:
                        dve.wait_ge(u_used, SLOTS * (j - 1))
                    tell(after().tensor_scalar(front[:, 1 + j % 2, :], xt, y8[:, 0:1], None, ALU.mult),
                         xn2_ready, j + 1)
                elif i == H2T:
                    for half in range(2):
                        dve.wait_ge(xn2T, 2 * j + half + 1)
                        for b in range(4):
                            k = 4 * half + b
                            last = v.tensor_scalar(h2T[:, k * P:(k + 1) * P], T[half][:, b * P:(b + 1) * P],
                                                   a2[:, k:k + 1], b2[:, k:k + 1], ALU.mult, ALU.add)
                        tell(last, h2T_ready, 2 * j + half + 1)
                elif i >= PEER + 5:
                    g, part = divmod(i - PEER - 5, 4)
                    (top_blocks_first, top_blocks_last, top_sums, pick)[part](j, g)

            def top16(rows):
                marks = [newest[0]] * len(rows)

                def each(make):
                    for n, row in enumerate(rows):
                        after(marks[n])
                        marks[n] = step(make(*row))

                each(lambda val, at, src, w: v.max(val[:, 0:8], src))
                each(lambda val, at, src, w: v.match_replace(out=w, in_to_replace=val[:, 0:8], in_values=src,
                                                             imm_value=TAKEN))
                each(lambda val, at, src, w: v.max_index(at[:, 0:8], val[:, 0:8], src))
                each(lambda val, at, src, w: v.max(val[:, 8:16], w))
                each(lambda val, at, src, w: v.max_index(at[:, 8:16], val[:, 8:16], w))

            def top_blocks(g, blocks):
                top16([(topv[:, 16 * b:16 * b + 16], topi[:, 16 * b:16 * b + 16], A[g % 2][:, b * P:(b + 1) * P],
                        wk[:, b * P:(b + 1) * P]) for b in blocks])

            def top_blocks_first(j, g):
                dve.wait_ge(pscores, 4 * j + g + 1)
                top_blocks(g, (0, 1))

            def top_blocks_last(j, g):
                top_blocks(g, (2, 3))
                tell(after().tensor_copy(topf[:, :], topi[:, :]), pscores_taken, 4 * j + g + 1)

            def top_sums(j, g):
                cand = lg[:, 0, :]
                for h in range(2):
                    f = topv[:, 32 * h:32 * h + 16].unsqueeze(2).broadcast_to([P, 16, 16])
                    s = topv[:, 32 * h + 16:32 * h + 32].unsqueeze(1).broadcast_to([P, 16, 16])
                    ins = v.tensor_tensor(cand[:, 256 * h:256 * h + 256].rearrange("p (a b) -> p a b", b=16), f, s, ALU.add)
                step(ins)
                at = 32 * g
                top16([(cval[:, at + 16 * h:at + 16 * h + 16], cpos[:, 16 * h:16 * h + 16],
                        cand[:, 256 * h:256 * h + 256], wk[:, 256 * h:256 * h + 256]) for h in range(2)])
                g3 = gates[:, j % 2, at:at + 32].rearrange("p (h k) -> p h k", h=2)
                c3 = cval[:, at:at + 32].rearrange("p (h k) -> p h k", h=2)
                tell(after().tensor_tensor(g3, c3, c3[:, :, 0:1].broadcast_to([P, 2, PK]), ALU.subtract),
                     gate_in, 4 * j + g + 1)

            def pick(j, g):
                one = lg[:, 1, :].rearrange("p (a b) -> p a b", b=16)
                iota = cst[:, C_IOTA:C_IOTA + 16].unsqueeze(1).broadcast_to([P, 32, 16])
                step(after().tensor_scalar(cpart[:, 0, :], cpos[:, :], 4, None, ALU.logical_shift_right))
                step(v.tensor_scalar(cpart[:, 1, :], cpos[:, :], 15, None, ALU.bitwise_and))
                for side in range(2):
                    step(after().tensor_tensor(one, cpart[:, side, :].unsqueeze(2).broadcast_to([P, 32, 16]), iota,
                                               ALU.is_equal))
                    after()
                    for h in range(2):
                        key = topf[:, 32 * h + 16 * side:32 * h + 16 * side + 16].unsqueeze(1).broadcast_to([P, 16, 16])
                        ins = v.tensor_tensor(one[:, 16 * h:16 * h + 16, :], one[:, 16 * h:16 * h + 16, :], key, ALU.mult)
                    step(ins)
                    step(after().reduce_sum(csel[:, side, :], one, AX_X))
                g3 = gates[:, j % 2, 32 * g:32 * g + 32].rearrange("p (h k) -> p h k", h=2)
                dve.wait_ge(gate_exp, 4 * j + g + 1)
                step(after().reduce_sum(gsum[:, 0:2], g3, AX_X))
                step(after().reciprocal(grec[:, 0:2], gsum[:, 0:2]))
                step(after().tensor_tensor(g3, g3, grec[:, 0:2].unsqueeze(2).broadcast_to([P, 2, PK]), ALU.mult))
                dve.wait_ge(h2_ready, 2 * j + 2)
                tell(after().scalar_tensor_tensor(out=eid[:, j % 2, 32 * g:32 * g + 32], in0=csel[:, 0, :], scalar=128.0,
                                                  in1=csel[:, 1, :], op0=ALU.mult, op1=ALU.add),
                     experts_ready, 4 * j + g + 1)

            for i in range(SPLIT):
                front_piece(0, i)
            for s in range(NT * SLOTS + PK + 1):
                n, k = divmod(s, PK)
                if s < NT * SLOTS:
                    j = s // SLOTS
                    dve.wait_ge(u_landed[s % NB], 16 * (s // NB + 1))
                    if k == 0 and n >= 2:
                        dve.wait_ge(gelu_done, n - 1)
                    buf = ubuf[s % NB]
                    v.scalar_tensor_tensor(out=buf, in0=buf, scalar=1.0, in1=front[:, 1 + j % 2, :], op0=ALU.mult,
                                           op1=ALU.mult, accum_out=dots[:, n % 2, k:k + 1]).then_inc(u_used, 1)
                if k == 0 and 1 <= n <= NT * PH:
                    m = n - 1
                    dve.wait_ge(gelu_done, m + 1)
                    if m >= 2:
                        dve.wait_ge(diag_ready, PK * (m - 1))
                    h = m % PH
                    v.tensor_tensor(wts[:, m % 2, :], gel[:, m % 2, :], gates[:, (m // PH) % 2, h * PK:(h + 1) * PK],
                                    ALU.mult).then_inc(wts_ready, 1)
                r = s - PK
                if r >= SLOTS and r % SLOTS == 0:
                    j = r // SLOTS - 1
                    dve.wait_ge(v_used, SLOTS * (j + 1))
                    dve.wait_ge(fin_loaded, 16 * (j + 1))
                    for half in range(2):
                        cut = slice(half * 512, (half + 1) * 512)
                        step(v.tensor_tensor(acc[half][:, :], acc[half][:, :], gate2[:, cut], ALU.mult))
                        ins = after().tensor_tensor(fin[:, cut], fin[:, cut], acc[half][:, :], ALU.add)
                        if half == 0:
                            step(ins)
                        else:
                            tell(ins, fin_ready, j + 1)
                for piece in behind.get(s, ()):
                    front_piece(*piece)


_INS = ["x", "c", "ada_w", "ada_b", "norm1_g", "w_in", "pool_w", "pool_scale", "pool_out_g", "q_norm_g",
        "k_norm_g", "attn_out_g", "w_out", "norm2_g", "peer_wq", "peer_subkeys", "peer_u", "peer_v"]


def kernel(**inputs):
    import numpy as _np
    import concourse.bacc as _bacc
    from concourse import mybir as _mybir
    from concourse.bass_utils import run_bass_kernel_spmd as _run

    nc = _bacc.Bacc("TRN2", target_bir_lowering=False, num_devices=1, dynamic_dma_scratch_size=8192)
    arrays, args = {}, []
    for name in _INS + ["const"]:
        a = constants() if name == "const" else _np.ascontiguousarray(inputs[name])
        arrays[f"in_{name}"] = a
        args.append(nc.dram_tensor(f"in_{name}", a.shape, _mybir.dt.from_np(a.dtype), kind="ExternalInput").ap())
    out = nc.dram_tensor("out_0", (1, SEQ, D), F32, kind="ExternalOutput").ap()
    hymba_block(nc, *args, out)
    r = _run(nc, [arrays], core_ids=[0])
    return r.results[0]["out_0"]
```

```python
from contextlib import ExitStack

import numpy as np

import concourse.bass as bass
from concourse import mybir

ALU = mybir.AluOpType
ACT = mybir.ActivationFunctionType
F32 = mybir.dt.float32
U32 = mybir.dt.uint32
AX_X = mybir.AxisListType.X

P = 128
D = 1024
KT = D // P
SEQ = 512
NT = SEQ // P
HEADS = 8
HD = 64
TOPK = 128
WIN = (2, 4, 8, 16)
EPS = 1e-6
MASKED = 1e30
TAKEN = -3e38
PH = 8
PK = 16
SLOTS = PH * PK
NB = 4
ITEM = [(ch, j) for ch in "uqk" for j in range(NT)] + [("ki", 0), ("wi", 0)] + [("v", j) for j in range(NT)]
ITEMS = len(ITEM)
AT_COLUMN = {"u": 0, "q": 512, "k": 1024, "v": 1536, "qi": 2048, "ki": 2560}

R_C, R_ADAB, R_N1, R_N2, R_OG, R_QG, R_KG, NROWS = 0, 8, 56, 64, 72, 80, 81, 82
C_ID, C_DIST, C_IOTA, C_HK, NCST = 0, 128, 640, 656, 672
IDX, TOP, ATT, END, PEER, PIECES = 0, 10, 27, 39, 50, 71
ATT_TURN, X2, XN2, H2_TURN, H2_MOD, H2_BACK = END + 2, END + 6, END + 7, END + 8, END + 9, END + 10
OUT_PROJ = (END, END + 1, END + 4, END + 5)
SPLIT = PEER + 9
QI_BEHIND = {X2: (0,), PEER + 7: (1, 2, 3)}
WEIGHT = [5] * TOP + [8] * (ATT - TOP) + [10] * (END - ATT) + [14] * (PEER - END) + [16] * (PIECES - PEER)


def constants():
    p = np.arange(P)[:, None].astype(np.float64)
    t = np.arange(P)[None, :].astype(np.float64)
    out = np.zeros((P, NCST + 12 * P))
    out[:, C_ID:C_ID + P] = p == t
    out[:, C_DIST:C_DIST + SEQ] = np.abs(p - (np.arange(SEQ)[None, :] - (SEQ - P)))
    out[:, C_IOTA:C_IOTA + 16] = np.arange(16)
    out[:, C_HK:C_HK + 8] = -(HD ** -0.5) * 2.0 ** np.arange(1, 9)
    out[:, C_HK + 8:C_HK + 16] = 1.0
    for g, w in enumerate(WIN):
        near = (p <= t) & (t - p < w)
        first = near / np.minimum(t + 1, w) - (p == t)
        later = near / w - (p == t)
        before = (t - (p - P) < w) / w
        for n, m in enumerate((first, later, before)):
            at = NCST + (n * 4 + g) * P
            out[:, at:at + P] = m
    return out.astype(np.float32)


def hymba_block(nc, x, c, ada_w, ada_b, norm1_g, w_in, pool_w, pool_scale, pool_out_g, q_norm_g,
                k_norm_g, attn_out_g, w_out, norm2_g, peer_wq, peer_subkeys, peer_u, peer_v, const,
                out):
    spill = nc.dram_tensor("spill", (NT, 3, P, SEQ), F32).ap()

    with ExitStack() as ctx:
        def sb(name, shape, dt=F32):
            return ctx.enter_context(nc.sbuf_tensor(name, shape, dt))

        def bank(name):
            return ctx.enter_context(nc.psum_tensor(name, [P, 512], F32))

        def sem(name):
            return ctx.enter_context(nc.semaphore(name))

        wq_sb = sb("wq_sb", [P, 4, KT, 512])
        wout_sb = sb("wout_sb", [P, KT, D])
        ring = sb("ring", [P, 2 * NB, D])
        keysT = sb("keysT", [P, 4, SEQ])
        vals = sb("vals", [P, NT, 512])
        kidxT = sb("kidxT", [P, SEQ])
        widx = sb("widx", [P, NT, 8])
        skT = sb("skT", [P, 16, P])
        tile_in = sb("tile_in", [P, 3, SEQ])
        front = sb("front", [P, 4, D])
        attT = sb("attT", [P, 512])
        gate2 = sb("gate2", [P, D])
        odd_x = sb("odd_x", [P, D])
        cst = sb("cst", [P, NCST])
        bias = sb("bias", [P, 512])
        score = sb("score", [P, 512])
        lg = sb("lg", [P, 2, 512])
        pr = sb("pr", [P, 2, 512])
        prT = sb("prT", [P, 2, 512])
        cols = sb("cols", [P, 96])
        modc = sb("modc", [P, 48])
        small = sb("small", [P, 128])
        topv = sb("topv", [P, 64])
        topi = sb("topi", [P, 64], U32)
        topf = sb("topf", [P, 64])
        wk = sb("wk", [P, 512])
        cval = sb("cval", [P, SLOTS])
        cpos = sb("cpos", [P, 32], U32)
        cpart = sb("cpart", [P, 2, 32], U32)
        csel = sb("csel", [P, 2, 32])
        eid = sb("eid", [P, 2, SLOTS], U32)
        gates = sb("gates", [P, 2, SLOTS])
        dots = sb("dots", [P, 2, PK])
        gel = sb("gel", [P, 2, PK])
        wts = sb("wts", [P, 2, PK])
        diag = sb("diag", [P, NB, P])

        A = [bank("A0"), bank("A1")]
        T = [bank("T0"), bank("T1")]
        B = [bank("B0"), bank("B1")]
        acc = [bank("acc0"), bank("acc1")]

        ident = cst[:, C_ID:C_ID + P]
        xts = [front[:, 0, :], odd_x[:, :]]
        h2T = front[:, 3, :]
        hT = ring[:, NB:2 * NB, :].rearrange("p a n -> p (a n)").rearrange("p (k t) -> p k t", k=KT)
        ubuf = [ring[:, b, :] for b in range(NB)]
        vbuf = [ring[:, NB + b, :] for b in range(NB)]

        room = wq_sb[:, :, :, :].rearrange("p g k n -> p (g k n)")
        x_all = room[:, 0:4096].rearrange("p (j n) -> p j n", j=NT)
        sk_raw = room[:, 0:2048].rearrange("p (b n) -> p b n", b=16)
        u_all = room[:, 8192:10240].rearrange("p (j n) -> p j n", j=NT)
        bands = room[:, 10240:11776].rearrange("p (b n) -> p b n", b=12)
        poolw = room[:, 11776:12288]
        pscale = room[:, 12288:12800]
        stage = room[:, 12800:14336].rearrange("p (b n) -> p b n", b=3)
        prm = room[:, 14336:14464]
        partial = room[:, 14464:15488].rearrange("p (b n) -> p b n", b=2)
        modcol = acc[1][:, 128:176]
        chunks = [ring[:, 0:4, :], front[:, :, :]]
        chunks = [a.rearrange("p a n -> p (a n)") for a in chunks] + [room[:, 4096:8192]]
        chunks = [a.rearrange("p (k n) -> p k n", k=KT) for a in chunks]
        chunks.append(odd_x[:, :].rearrange("p (k n) -> p k n", k=KT))
        chunks.append(room[:, 8192:12288].rearrange("p (k n) -> p k n", k=KT))
        square = pr
        normed = prT
        pooled_sb = lg[:, 0, :]
        pool_n = lg[:, 1, :]
        gate1 = [wk[:, :], attT[:, :]]

        ones = sb("ones", [P, P])
        scol = modc[:, 0:8]
        a1, b1, a2, b2 = (modc[:, 8 + 8 * n:16 + 8 * n] for n in range(4))
        ecol = modc[:, 40:48]
        ss8, var8, y8, t8 = (small[:, 8 * n:8 * n + 8] for n in range(4))
        m8, mn8, rs8, rr8 = (small[:, 32 + 8 * n:40 + 8 * n] for n in range(4))
        ssx, gsum, grec = small[:, 64:68], small[:, 72:80], small[:, 80:88]
        sspool = small[:, 68:72]

        rows_in = sem("rows_in")
        cst_in = sem("cst_in")
        x_in = [sem(f"x_in{j}") for j in range(NT)]
        chunk_in = [sem(f"chunk_in{b}") for b in range(5)]
        pool_in = sem("pool_in")
        sk_in = sem("sk_in")
        wout_in = sem("wout_in")
        wq_in = [sem(f"wq_in{g}") for g in range(4)]
        tile_loaded = sem("tile_loaded")
        xt_loaded = [sem(f"xt_loaded{b}") for b in range(2)]
        out_saved = sem("out_saved")
        kidx_twice = sem("kidx_twice")
        qi_saved = [sem(f"qi_saved{b}") for b in range(2)]
        spilled = [sem(f"spilled{b}") for b in range(3)]
        u_landed = [sem(f"u_landed{b}") for b in range(NB)]
        v_landed = [sem(f"v_landed{b}") for b in range(NB)]
        rowsT_ready = sem("rowsT_ready")
        cols_ready = sem("cols_ready")
        exp_c = sem("exp_c")
        scol_ready = sem("scol_ready")
        mod_taken = sem("mod_taken")
        xss_ready = sem("xss_ready")
        x_scale_ready = sem("x_scale_ready")
        xn_ready = sem("xn_ready")
        hT_ready = sem("hT_ready")
        turned = sem("turned")
        turn_taken = sem("turn_taken")
        projected = sem("projected")
        item_squared = sem("item_squared")
        item_taken = [sem(f"item_taken{b}") for b in range(2)]
        normed_ready = [sem(f"normed_ready{b}") for b in range(2)]
        partial_ready = [sem(f"partial_ready{b}") for b in range(2)]
        modcol_ready = sem("modcol_ready")
        poolw_ready = sem("poolw_ready")
        pooled = sem("pooled")
        pooled_taken = sem("pooled_taken")
        mixed = sem("mixed")
        mixed_squared = sem("mixed_squared")
        mixed_taken = sem("mixed_taken")
        qi_done = sem("qi_done")
        qi_taken = sem("qi_taken")
        gains_in = sem("gains_in")
        wout_gated = sem("wout_gated")
        gate_bias_in = sem("gate_bias_in")
        row_taken = sem("row_taken")
        dotted = sem("dotted")
        relu_done = sem("relu_done")
        relu_used = sem("relu_used")
        logits = sem("logits")
        biased = sem("biased")
        expd = sem("expd")
        probT = sem("probT")
        probT_taken = sem("probT_taken")
        pv_done = sem("pv_done")
        att_read = sem("att_read")
        att_ready = sem("att_ready")
        attT_ready = sem("attT_ready")
        attT_taken = sem("attT_taken")
        out_proj = sem("out_proj")
        x2_ready = sem("x2_ready")
        x2_squared = sem("x2_squared")
        xn2_ready = sem("xn2_ready")
        xn2T = sem("xn2T")
        h2T_ready = sem("h2T_ready")
        h2_turned = sem("h2_turned")
        h2_ready = sem("h2_ready")
        pq_done = sem("pq_done")
        pq_taken = sem("pq_taken")
        pscores = sem("pscores")
        pscores_taken = sem("pscores_taken")
        gate_in = sem("gate_in")
        gate_exp = sem("gate_exp")
        experts_ready = sem("experts_ready")
        u_used = sem("u_used")
        v_used = sem("v_used")
        gelu_done = sem("gelu_done")
        wts_ready = sem("wts_ready")
        diag_ready = sem("diag_ready")
        fin_ready = sem("fin_ready")
        dve_step = sem("dve_step")
        act_step = sem("act_step")
        pool_step = sem("pool_step")

        stream = [("ada", 0, 2), ("ada", 1, 0), ("ada", 2, 1), ("ada", 3, 2), ("in", "u", 0), ("in", "q", 1),
                  ("ada", 4, 2), ("in", "ki", 3), ("ada", 5, 2), ("in", "k", 0), ("ada", 6, 2), ("ada", 7, 1),
                  ("ada", 8, 2), ("in", "v", 1), ("ada", 9, 2), ("ada", 10, 0), ("ada", 11, 2), ("in", "qi", 4)]
        in_buffer = {b: [(kind, m) for kind, m, o in stream if o == b] for b in range(5)}
        at_stream = {(kind, m): (b, in_buffer[b].index((kind, m)) + 1) for kind, m, b in stream}
        BY_POOL = (6, 7, 8)
        DVE_ADA_AT = {0: 4, 1: 5, 12: 9, 13: 10, 15: 11}
        ADA_AT = {2: 4, 6: 5, 8: 6, 10: 7, 12: 8, 14: 9, 15: 10, 16: 11}
        GAINS_AT = 6
        GATES = (4, 5, 10, 11)
        ROW_AT = {3: 0, 8: 1, 16: 2, 18: 3}
        MODS_AT = 15
        TURN_X = 2 * NT

        def item(i):
            return ITEM[i]

        def items_until(ch):
            return max(i for i in range(ITEMS) if item(i)[0] == ("wi" if ch == "ki" else ch)) + 1

        def chunk_loaded(eng, kind, m):
            b, count = at_stream[kind, m]
            eng.wait_ge(chunk_in[b], 16 * count)
            return chunks[b]

        def partial_made(eng, a):
            eng.wait_ge(partial_ready[a % 2], a // 2 + 1)

        def is_turned(i):
            return 0 <= i < ITEMS and item(i)[0] in ("q", "k")

        def normed_count(i):
            return sum(is_turned(m) for m in range(i % 2, i + 1, 2))

        def taken_count(i):
            return sum(item(m)[0] in ("u", "ki", "wi", "v") for m in range(i % 2, i + 1, 2))

        def item_left(eng, i):
            if is_turned(i):
                eng.wait_ge(normed_ready[i % 2], normed_count(i))
            else:
                eng.wait_ge(item_taken[i % 2], taken_count(i))

        def pooled_at(i):
            return (i - 2) // 2 if i in (2, 4, 6, 8) else None

        def mix_at(i):
            return (i - 3) // 2 if i in (3, 5, 7, 9) else None

        def poolturn_at(i):
            return (i - 4) // 2 if i in (4, 6, 8, 10) else None

        def keys_at(i):
            return i - 14 if 14 <= i < 18 else None

        turn_plan, turn_step = [], []
        for i in range(ITEMS + 2):
            if is_turned(i - 1):
                turn_plan.append((item(i - 1)[0], item(i - 1)[1]))
            if poolturn_at(i) is not None:
                turn_plan.append(("pool", poolturn_at(i)))
            if keys_at(i) is not None:
                turn_plan.append(("keys", keys_at(i)))
            turn_step += [i] * (len(turn_plan) - len(turn_step))

        def turns_before(i):
            n = len([m for m in range(i - 1) if is_turned(m)])
            items = [t for t, (ch, _) in enumerate(turn_plan) if ch in ("q", "k")]
            return TURN_X + items[n - 1] + 1

        stage_plan = [(ch, j) for ch, j in turn_plan if ch in ("q", "pool")]
        SLAB = {"q": 0, "pool": 2}
        TURNS = TURN_X + len(turn_plan)

        def keys_of(j):
            return (j + 1) * P

        behind = {}
        late_at = (6, 12, 18, 24, 28, 32, 36, 40, 44, 48, 52, 56)
        for n in range(SPLIT, PIECES):
            behind[late_at[n - SPLIT]] = [(0, n)]
        for j in range(1, NT):
            for n in range(PIECES):
                if j == 1 and n < SPLIT:
                    s_at = 58 + (SLOTS - 3 - 58) * sum(WEIGHT[:n]) // sum(WEIGHT[:SPLIT])
                else:
                    s_at = SLOTS * j - 3 + SLOTS * (sum(WEIGHT[:n]) - sum(WEIGHT[:SPLIT])) // sum(WEIGHT)
                behind.setdefault(s_at, []).append((j, n))

        block = ctx.enter_context(nc.Block())

        @block.sync
        def _(sp):
            rows = [(R_C, c.rearrange("a (r n) -> (a r) n", n=P), 8),
                    (R_ADAB, ada_b.rearrange("a (r n) -> (a r) n", n=P), 48),
                    (R_N1, norm1_g.rearrange("a (r n) -> (a r) n", n=P), 8),
                    (R_N2, norm2_g.rearrange("a (r n) -> (a r) n", n=P), 8),
                    (R_OG, pool_out_g.rearrange("a (r n) -> (a r) n", n=P), 4),
                    (R_OG + 4, attn_out_g.rearrange("a (r b) n -> (a r) (b n)", b=2), 4)]
            for at, src, n in rows:
                sp.dma_start(prm[at:at + n, :], src).then_inc(rows_in, 16)
            for half in range(2):
                for at, g in ((R_QG, q_norm_g), (R_KG, k_norm_g)):
                    sp.dma_start(prm[at:at + 1, half * HD:half * HD + HD], g).then_inc(rows_in, 16)
            sp.dma_start(cst[:, :], const[:, 0:NCST]).then_inc(cst_in, 16)
            for j in range(NT):
                sp.dma_start(x_all[:, j, :], x[0, j * P:(j + 1) * P, :]).then_inc(x_in[j], 16)

            def load_chunk(n):
                kind, m, b = stream[n]
                before = in_buffer[b][:at_stream[kind, m][1] - 1]
                if before:
                    was, o = before[-1]
                    sp.wait_ge(*((partial_ready[o % 2], o // 2 + 1) if was == "ada" else (projected, items_until(o))))
                if m == "qi":
                    sp.wait_ge(mixed, NT)
                at = m * 512 if kind == "ada" else AT_COLUMN[m]
                table = (ada_w if kind == "ada" else w_in)[0].rearrange("(k p) n -> p k n", p=P)
                w = HD + 8 if m == "ki" else 512
                sp.dma_start(chunks[b][:, :, 0:w], table[:, :, at:at + w]).then_inc(chunk_in[b], 16)

            for n in range(3):
                load_chunk(n)
            load_chunk(3)
            load_chunk(4)
            sp.dma_start(bands, const[:, NCST:].rearrange("p (b n) -> p b n", b=12)).then_inc(pool_in, 16)
            sp.dma_start(poolw, pool_w[0].rearrange("g c d -> c g d")).then_inc(pool_in, 16)
            sp.dma_start(pscale, pool_scale[0:1, :].broadcast_to([P, 512])).then_inc(pool_in, 16)
            for half in range(2):
                for row, at in ((gate1[half], 2 * D), (gate2[:, half * 512:(half + 1) * 512], 5 * D)):
                    sp.dma_start(row, ada_b[0:1, at + 512 * half:at + 512 * half + 512].broadcast_to([P, 512])).then_inc(gate_bias_in, 16)
            for n in range(5, 8):
                load_chunk(n)
            sp.wait_ge(turned, TURN_X)
            sp.dma_start(sk_raw, peer_subkeys[0].rearrange("h s n d -> n (h s) d")).then_inc(sk_in, 16)
            for n in range(8, len(stream)):
                load_chunk(n)
                if stream[n][1] == 6:
                    sp.dma_start(wout_sb[:, :, :], w_out[0].rearrange("(k p) n -> p k n", p=P)).then_inc(wout_in, 16)

            def load_queries(j):
                if j == 0:
                    for b in range(3):
                        sp.wait_ge(spilled[b], 16 * len(stage_plan[b::3]))
                    for n in (0, 2):
                        sp.dma_start(tile_in[:, n, :], spill[0, n]).then_inc(tile_loaded, 16)
                    return
                sp.wait_ge(out_proj, j)
                sp.dma_start(tile_in[:, :, :], spill[j].rearrange("a p n -> p a n")).then_inc(tile_loaded, 16)

            def load_x(j):
                if j == 0:
                    sp.wait_ge(projected, ITEMS)
                elif j == 1:
                    for b in range(2):
                        sp.wait_ge(qi_saved[b], 32)
                else:
                    sp.wait_ge(out_saved, 16 * (j - 1))
                sp.dma_start(xts[j % 2], x[0, j * P:(j + 1) * P, :]).then_inc(xt_loaded[j % 2], 16)

            wq_v = peer_wq[0].rearrange("(k p) n -> p k n", p=P)

            def load_wq(g):
                sp.dma_start(wq_sb[:, g, :, :], wq_v[:, :, g * 512:(g + 1) * 512]).then_inc(wq_in[g], 16)

            load_queries(0)
            item_left(sp, ITEM.index(("wi", 0)))
            sp.dma_start(kidxT[HD:P, :], kidxT[0:HD, :]).then_inc(kidx_twice, 16)
            sp.wait_ge(modcol_ready, 12)
            load_wq(3)
            sp.wait_ge(turned, TURNS)
            load_wq(0)
            load_x(0)
            load_wq(1)

            sp.wait_ge(qi_done, 4)
            load_wq(2)
            load_x(1)
            load_queries(1)
            for j in range(NT):
                if 1 <= j < NT - 1:
                    load_queries(j + 1)
                sp.wait_ge(fin_ready, j + 1)
                sp.dma_start(out[0, j * P:(j + 1) * P, :], xts[j % 2]).then_inc(out_saved, 16)
                if j + 2 < NT:
                    load_x(j + 2)
            sp.wait_ge(out_saved, 16 * NT)

        @block.gpsimd
        def _(pool):
            steps = 0
            pool.wait_ge(scol_ready, 1)
            for a in BY_POOL:
                w = chunk_loaded(pool, "ada", a)
                if a >= 2:
                    pool.wait_ge(modcol_ready, a - 1)
                nc.gpsimd.tensor_tensor(w, w, scol.unsqueeze(2).broadcast_to([P, KT, 512]), ALU.mult).then_inc(pool_step, 1)
                for half in (4, 2, 1):
                    steps += 1
                    pool.wait_ge(pool_step, steps)
                    o = w[:, 0:half, :] if half > 1 else partial[:, a % 2:a % 2 + 1, :]
                    nc.gpsimd.tensor_tensor(o, w[:, 0:half, :], w[:, half:2 * half, :], ALU.add).then_inc(
                        pool_step if half > 1 else partial_ready[a % 2], 1)

            for half in range(2):
                pool.wait_ge(row_taken, half + 1)
                pool.wait_ge(gains_in, KT)
                w = wout_sb[:, :, half * 512:(half + 1) * 512]
                nc.gpsimd.tensor_tensor(w, w, gate1[half].unsqueeze(1).broadcast_to([P, KT, 512]),
                                        ALU.mult).then_inc(wout_gated, 1)

            def gather(table, buf, landed, used, s):
                if s >= NB:
                    pool.wait_ge(used, s - NB + 1)
                    pool.wait_ge(landed[s % NB], 16 * (s // NB))
                j, r = divmod(s, SLOTS)
                pool.indirect_dma_start(
                    buf[s % NB], None, table,
                    bass.IndirectOffsetOnAxis(ap=eid[:, j % 2, r:r + 1], axis=0),
                ).then_inc(landed[s % NB], 16)

            pool.wait_ge(projected, ITEMS)
            pool.wait_ge(partial_ready[1], 6)
            for s in range(NT * SLOTS + PK):
                if s < NT * SLOTS:
                    if s % (2 * PK) == 0:
                        pool.wait_ge(experts_ready, s // (2 * PK) + 1)
                    gather(peer_u[0], ubuf, u_landed, u_used, s)
                if s == PK:
                    pool.wait_ge(qi_done, 4)
                if s >= PK:
                    gather(peer_v[0], vbuf, v_landed, v_used, s - PK)

        @block.tensor
        def _(pe):
            mm = nc.tensor.matmul
            pe.wait_ge(rows_in, 16 * 10)
            pe.wait_ge(cst_in, 16)
            nc.tensor.transpose(acc[1][:, 0:NROWS], prm[0:NROWS, :], ident[0:NROWS, 0:NROWS]).then_inc(rowsT_ready, 1)

            def ada_sum(a):
                partial_made(pe, a)
                if a in GATES:
                    if GATES.index(a) >= 1:
                        pe.wait_ge(row_taken, GATES.index(a))
                    last = mm(acc[0][:, :], ones[:, :], partial[:, a % 2, :], start=True, stop=True)
                else:
                    for b in range(4):
                        last = mm(modcol[:, 4 * a + b:4 * a + b + 1], partial[:, a % 2, b * P:(b + 1) * P], ones[:, 0:1],
                                  start=True, stop=True)
                last.then_inc(modcol_ready, 1)

            def turn_bank(n, src, blocks=4):
                if n >= 2:
                    pe.wait_ge(turn_taken, n - 1)
                for b in range(blocks):
                    last = nc.tensor.transpose(T[n % 2][:, b * P:(b + 1) * P], src[:, b * P:(b + 1) * P], ident)
                last.then_inc(turned, 1)

            for j in range(NT):
                pe.wait_ge(xn_ready, j + 1)
                for half in range(2):
                    turn_bank(2 * j + half, x_all[:, j, half * 512:(half + 1) * 512])

            pe.wait_ge(cols_ready, 1)
            for a in range(4):
                ada_sum(a)

            turns = TURN_X
            for i in range(ITEMS + 2):
                if i < ITEMS:
                    ch, j = item(i)
                    if ch != "wi":
                        w = chunk_loaded(pe, "in", ch)
                    if i >= 2:
                        item_left(pe, i - 2)
                    if ch == "wi":
                        item_left(pe, i - 1)
                        for t in range(NT):
                            last = nc.tensor.transpose(A[i % 2][:, 8 * t:8 * t + 8], kidxT[HD:HD + 8, t * P:(t + 1) * P],
                                                       ident[HD:HD + 8, HD:HD + 8])
                    else:
                        for k in range(KT):
                            if i == 0:
                                pe.wait_ge(hT_ready, k + 1)
                            if ch == "ki":
                                o, mine, every = A[i % 2][0:HD + 8, :], w[:, k, 0:HD + 8], hT[:, k, :]
                            else:
                                o, mine, every = A[i % 2][:, :], hT[:, k, j * P:(j + 1) * P], w[:, k, :]
                            last = mm(o, mine, every, start=(k == 0), stop=(k == KT - 1))
                    last.then_inc(projected, 1)
                if i - 1 in ADA_AT:
                    ada_sum(ADA_AT[i - 1])
                if is_turned(i - 1):
                    pe.wait_ge(normed_ready[(i - 1) % 2], normed_count(i - 1))
                    turn_bank(turns, normed[:, (i - 1) % 2, :])
                    turns += 1
                if (j := pooled_at(i)) is not None:
                    pe.wait_ge(pool_in, 48)
                    pe.wait_ge(item_taken[j % 2], j // 2 + 1)
                    if j >= 1:
                        pe.wait_ge(pooled_taken, j)
                    for g in range(4):
                        o = B[0][:, g * P:(g + 1) * P]
                        last = mm(o, u_all[:, j, g * P:(g + 1) * P], bands[:, g if j == 0 else 4 + g, :],
                                  start=True, stop=(j == 0))
                        if j >= 1:
                            last = mm(o, u_all[:, j - 1, g * P:(g + 1) * P], bands[:, 8 + g, :], start=False, stop=True)
                    last.then_inc(pooled, 1)
                if (j := mix_at(i)) is not None:
                    pe.wait_ge(pooled_taken, j + 1)
                    pe.wait_ge(poolw_ready, 1)
                    if j >= 1:
                        pe.wait_ge(mixed_taken, j)
                    for g in range(4):
                        last = mm(B[1][:, g * P:(g + 1) * P], pooled_sb[:, g * P:(g + 1) * P],
                                  poolw[:, g * P:(g + 1) * P], start=True, stop=True)
                    last.then_inc(mixed, 1)
                if (j := poolturn_at(i)) is not None:
                    pe.wait_ge(mixed_taken, j + 1)
                    turn_bank(turns, pool_n)
                    turns += 1
                if keys_at(i) is not None:
                    g = keys_at(i)
                    pe.wait_ge(sk_in, 16)
                    turn_bank(turns, sk_raw[:, 4 * g:4 * g + 4, :].rearrange("p b n -> p (b n)"))
                    turns += 1

            def front_piece(j, i):
                W = keys_of(j)
                qT, qiT, plT = (tile_in[:, n, :] for n in range(3))
                if i < TOP:
                    if j == 0 or i >= 8:
                        return
                    if i == 0:
                        pe.wait_ge(tile_loaded, 16 * (j + 2))
                        pe.wait_ge(pscores_taken, 4 * j)
                    if i >= 2:
                        pe.wait_ge(relu_done, 8 * (j - 1) + i - 1)
                    o = HD * (i % 2)
                    pe.wait_ge(kidx_twice, 16)
                    mm(A[i % 2][:, 0:W], qiT[o:o + HD, (i // 2) * P:(i // 2 + 1) * P], kidxT[o:o + HD, 0:W],
                       start=True, stop=True).then_inc(dotted, 1)
                elif ATT <= i < END:
                    h = i - ATT
                    if h < HEADS:
                        if h == 0:
                            if j == 0:
                                item_left(pe, ITEMS - 2)
                                item_left(pe, ITEMS - 1)
                                pe.wait_ge(tile_loaded, 32)
                            else:
                                pe.wait_ge(relu_done, 8 * j)
                        if h >= 2:
                            pe.wait_ge(biased, 8 * j + h - 1)
                        o = HD * (h % 2)
                        mm(A[h % 2][:, 0:W], qT[o:o + HD, (h // 2) * P:(h // 2 + 1) * P], keysT[o:o + HD, h // 2, 0:W],
                           start=True, stop=True).then_inc(logits, 1)
                    if 2 <= h < HEADS + 2:
                        h -= 2
                        pe.wait_ge(expd, 8 * j + h + 1)
                        if h < 2:
                            pe.wait_ge(turn_taken, TURNS)
                            if j >= 1:
                                pe.wait_ge(h2_ready, 2 * j)
                        else:
                            pe.wait_ge(probT_taken, 8 * j + h - 1)
                        for b in range(j + 1):
                            last = nc.tensor.transpose(T[h % 2][:, b * P:(b + 1) * P], pr[:, h % 2, b * P:(b + 1) * P], ident)
                        last.then_inc(probT, 1)
                        h += 2
                    if h >= 4:
                        h -= 4
                        pe.wait_ge(probT_taken, 8 * j + h + 1)
                        if h == 0 and j >= 1:
                            pe.wait_ge(att_read, j)
                        for b in range(j + 1):
                            last = mm(B[0][:, h * HD:(h + 1) * HD], prT[:, h % 2, b * P:(b + 1) * P],
                                      vals[:, b, h * HD:(h + 1) * HD], start=(b == 0), stop=(b == j))
                        last.then_inc(pv_done, 1)
                elif i == ATT_TURN:
                    pe.wait_ge(att_ready, j + 1)
                    pe.wait_ge(probT_taken, 8 * j + 8)
                    for b in range(4):
                        last = nc.tensor.transpose(T[0][:, b * P:(b + 1) * P], score[:, b * P:(b + 1) * P], ident)
                    last.then_inc(attT_ready, 1)
                elif i in OUT_PROJ:
                    part = OUT_PROJ.index(i)
                    if part == 0:
                        pe.wait_ge(biased, 8 * j + 8)
                        pe.wait_ge(wout_gated, 2)
                    if part == 2:
                        pe.wait_ge(attT_taken, j + 1)
                    for k in (2 * part, 2 * part + 1):
                        src = plT[:, k * P:(k + 1) * P] if k < 4 else attT[:, (k - 4) * P:(k - 3) * P]
                        for half in range(2):
                            last = mm(A[half][:, :], src, wout_sb[:, k, half * 512:(half + 1) * 512],
                                      start=(k == 0), stop=(k == KT - 1))
                    if part == 3:
                        last.then_inc(out_proj, 1)
                elif i == H2_TURN:
                    pe.wait_ge(xn2_ready, j + 1)
                    for b in range(KT):
                        last = nc.tensor.transpose(T[b // 4][:, (b % 4) * P:(b % 4 + 1) * P],
                                                   front[:, 1 + j % 2, b * P:(b + 1) * P], ident)
                        if b % 4 == 3:
                            last.then_inc(xn2T, 1)
                elif i == H2_BACK:
                    for half in range(2):
                        pe.wait_ge(h2T_ready, 2 * j + half + 1)
                        for b in range(4):
                            k = 4 * half + b
                            last = nc.tensor.transpose(T[half][:, b * P:(b + 1) * P], h2T[:, k * P:(k + 1) * P], ident)
                        last.then_inc(h2_turned, 1)
                elif i >= PEER:
                    g, b = divmod(i - PEER, 4)
                    if b == 0 and 1 <= g <= 4:
                        n = 4 * j + g - 1
                        pe.wait_ge(pq_taken, n + 1)
                        if g - 1 < 2:
                            pe.wait_ge(x2_ready, j + 1)
                        else:
                            pe.wait_ge(pscores_taken, n - 1)
                        for m in range(4):
                            last = mm(A[(g - 1) % 2][:, m * P:(m + 1) * P], prT[:, 0, m * P:(m + 1) * P],
                                      skT[:, 4 * (g - 1) + m, :], start=True, stop=True)
                        last.then_inc(pscores, 1)
                    if g < 4:
                        if b == 0:
                            pe.wait_ge(wq_in[g], 16)
                            pe.wait_ge(h2T_ready, 2 * j + 2)
                            if 4 * j + g >= 1:
                                pe.wait_ge(pq_taken, 4 * j + g)
                        for k in range(KT):
                            last = mm(B[1][:, b * P:(b + 1) * P], wq_sb[:, g, k, b * P:(b + 1) * P],
                                      h2T[:, k * P:(k + 1) * P], start=(k == 0), stop=(k == KT - 1))
                        if b == 3:
                            last.then_inc(pq_done, 1)

            def qi_block(b):
                w = chunk_loaded(pe, "in", "qi")
                if b == 0:
                    pe.wait_ge(row_taken, 4)
                    pe.wait_ge(mod_taken, 1)
                if b >= 2:
                    pe.wait_ge(qi_taken, b - 1)
                for k in range(KT):
                    last = mm(acc[b % 2][:, 0:SEQ - P], w[:, k, b * P:(b + 1) * P], hT[:, k, P:SEQ],
                              start=(k == 0), stop=(k == KT - 1))
                last.then_inc(qi_done, 1)

            for i in range(SPLIT):
                front_piece(0, i)
                for b in QI_BEHIND.get(i, ()):
                    qi_block(b)
            for s in range(NT * SLOTS + PK):
                m = s - PK
                if m >= 0:
                    j, r = divmod(m, SLOTS)
                    if r == 0 and j == 0:
                        pe.wait_ge(qi_taken, 4)
                    if r == 0 and j >= 1:
                        pe.wait_ge(fin_ready, j)
                    pe.wait_ge(diag_ready, m + 1)
                    pe.wait_ge(v_landed[m % NB], 16 * (m // NB + 1))
                    for half in range(2):
                        last = mm(acc[half][:, :], diag[:, m % NB, :], vbuf[m % NB][:, half * 512:(half + 1) * 512],
                                  start=(r == 0), stop=(r == SLOTS - 1))
                    last.then_inc(v_used, 1)
                for piece in behind.get(s, ()):
                    front_piece(*piece)

        @block.scalar
        def _(act):
            steps = [0]

            def link(ins):
                steps[0] += 1
                ins.then_inc(act_step, 1)
                act.wait_ge(act_step, steps[0])

            fn = nc.scalar.activation
            act.wait_ge(cols_ready, 1)
            fn(ecol, cols[:, R_C:R_C + 8], ACT.Exp, scale=-1.0).then_inc(exp_c, 1)
            for j in range(NT):
                act.wait_ge(x_in[j], 16)
                if j >= 2:
                    act.wait_ge(xss_ready, j - 1)
                fn(u_all[:, 2 * (j % 2):2 * (j % 2) + 2, :].rearrange("p a n -> p (a n)"), x_all[:, j, :], ACT.Square,
                   accum_out=ssx[:, j:j + 1]).then_inc(xss_ready, 1)
            act.wait_ge(xss_ready, NT)
            act.wait_ge(x_scale_ready, 1)
            for j in range(NT):
                fn(x_all[:, j, :], x_all[:, j, :], ACT.Copy, scale=y8[:, j:j + 1]).then_inc(xn_ready, 1)
            for n in range(TURN_X):
                act.wait_ge(turned, n + 1)
                j, half = divmod(n, 2)
                fn(hT[:, 4 * half:4 * half + 4, j * P:(j + 1) * P], T[n % 2][:, :].rearrange("p (k n) -> p k n", k=4),
                   ACT.Copy).then_inc(turn_taken, 1)

            staged_at = [t for t, (ch, _) in enumerate(turn_plan) if ch in ("q", "pool")]

            def save_staged(step):
                for e, t in enumerate(staged_at):
                    if turn_step[t] == step:
                        what, j = stage_plan[e]
                        act.wait_ge(turn_taken, TURN_X + t + 1)
                        act.dma_start(spill[j, SLAB[what]], stage[:, e % 3, :]).then_inc(spilled[e % 3], 16)

            for i in range(ITEMS):
                ch, j = item(i)
                act.wait_ge(projected, i + 1)
                src = A[i % 2][:, 0:512]
                if ch == "u":
                    fn(u_all[:, j, :], src, ACT.Copy).then_inc(item_taken[i % 2], 1)
                elif ch in ("q", "k"):
                    if normed_count(i) > 1:
                        act.wait_ge(normed_ready[i % 2], normed_count(i) - 1)
                    fn(square[:, i % 2, :], src, ACT.Square).then_inc(item_squared, 1)
                elif ch == "v":
                    fn(vals[:, j, :], src, ACT.Copy).then_inc(item_taken[i % 2], 1)
                elif ch == "ki":
                    fn(kidxT[0:HD + 8, :], A[i % 2][0:HD + 8, :], ACT.Copy).then_inc(item_taken[i % 2], 1)
                else:
                    fn(widx[:, :, :].rearrange("p j h -> p (j h)"), src[:, 0:8 * NT], ACT.Copy,
                       scale=float(np.float32(8 ** -0.5)) * HD ** -0.5).then_inc(item_taken[i % 2], 1)
                if (t := pooled_at(i)) is not None:
                    act.wait_ge(pooled, t + 1)
                    if t >= 1:
                        act.wait_ge(mixed_taken, t)
                    fn(pooled_sb, B[0][:, :], ACT.Copy).then_inc(pooled_taken, 1)
                if (t := mix_at(i)) is not None:
                    act.wait_ge(mixed, t + 1)
                    fn(pooled_sb, B[1][:, :], ACT.Square, accum_out=sspool[:, t:t + 1]).then_inc(mixed_squared, 1)
                save_staged(i - 1)
                if GAINS_AT <= i < GAINS_AT + 8:
                    k = i - GAINS_AT
                    act.wait_ge(wout_in, 16)
                    fn(wout_sb[:, k, :], wout_sb[:, k, :], ACT.Copy,
                       scale=cols[:, R_OG + k:R_OG + k + 1]).then_inc(gains_in, 1)

            def front_piece(j, i):
                W = keys_of(j)
                if i < TOP:
                    i -= 1
                    if j == 0 or not 0 <= i < 8:
                        return
                    n = 8 * (j - 1) + i
                    act.wait_ge(dotted, n + 1)
                    if i >= 2:
                        act.wait_ge(relu_used, n - 1)
                    else:
                        act.wait_ge(probT, 8 * j)
                        if n >= 2:
                            act.wait_ge(relu_used, n - 1)
                    fn(pr[:, i % 2, 0:W], A[i % 2][:, 0:W], ACT.Relu).then_inc(relu_done, 1)
                elif ATT <= i < END:
                    h = i - ATT - 1
                    if 0 <= h < HEADS:
                        n = 8 * j + h
                        act.wait_ge(biased, n + 1)
                        if n >= 2:
                            act.wait_ge(probT, n - 1)
                        if h < 2 and j >= 1:
                            act.wait_ge(relu_used, 8 * j)
                        fn(pr[:, h % 2, 0:W], lg[:, h % 2, 0:W], ACT.Exp, bias=mn8[:, h:h + 1], scale=-1.0,
                           accum_out=rs8[:, h:h + 1]).then_inc(expd, 1)
                    h -= 2
                    if 0 <= h < HEADS:
                        n = 8 * j + h
                        act.wait_ge(probT, n + 1)
                        if h < 2 and j >= 1:
                            act.wait_ge(pscores, 4 * j)
                        if n >= 2:
                            act.wait_ge(pv_done, n - 1)
                        fn(prT[:, h % 2, 0:W], T[h % 2][:, 0:W], ACT.Copy).then_inc(probT_taken, 1)
                elif i == ATT_TURN + 1:
                    if j == 0:
                        act.wait_ge(wout_gated, 2)
                    act.wait_ge(attT_ready, j + 1)
                    if j >= 1:
                        act.wait_ge(out_proj, j)
                    fn(attT[:, :], T[0][:, :], ACT.Copy).then_inc(attT_taken, 1)
                elif i == X2:
                    act.wait_ge(x2_ready, j + 1)
                    if j >= 1:
                        act.wait_ge(pq_done, 4 * j)
                    fn(h2T, xts[j % 2], ACT.Square, accum_out=ssx[:, 0:1]).then_inc(x2_squared, 1)
                elif i == H2_BACK + 1:
                    for half in range(2):
                        act.wait_ge(h2_turned, 2 * j + half + 1)
                        fn(front[:, 1 + j % 2, half * 512:(half + 1) * 512], T[half][:, :], ACT.Copy).then_inc(h2_ready, 1)
                elif i >= PEER:
                    g, b = divmod(i - PEER, 4)
                    if b == 3 and g >= 1:
                        act.wait_ge(gate_in, 4 * j + g)
                        g2 = gates[:, j % 2, 32 * (g - 1):32 * g]
                        fn(g2, g2, ACT.Exp).then_inc(gate_exp, 1)
                    if b == 3 and g < 4:
                        act.wait_ge(pq_done, 4 * j + g + 1)
                        if g == 0:
                            act.wait_ge(pv_done, 8 * j + 8)
                        else:
                            act.wait_ge(pscores, 4 * j + g)
                        fn(prT[:, 0, :], B[1][:, :], ACT.Copy).then_inc(pq_taken, 1)

            def qi_block(b):
                act.wait_ge(qi_done, b + 1)
                if b >= 2:
                    act.wait_ge(qi_saved[b % 2], 16)
                o = odd_x[:, 512 * (b % 2):512 * (b % 2) + SEQ - P]
                fn(o, acc[b % 2][:, 0:SEQ - P], ACT.Copy).then_inc(qi_taken, 1)
                act.wait_ge(qi_taken, b + 1)
                act.dma_start(spill[1:NT, 1, :, b * P:(b + 1) * P].rearrange("j p n -> p j n"),
                              o.rearrange("p (j n) -> p j n", n=P)).then_inc(qi_saved[b % 2], 16)

            for i in range(SPLIT):
                front_piece(0, i)
                for b in QI_BEHIND.get(i, ()):
                    qi_block(b)
            for s in range(NT * SLOTS + PK):
                m = s - PK
                n, k = divmod(s, PK)
                if k == 0 and n >= 1:
                    act.wait_ge(u_used, PK * n)
                    if n >= 3:
                        act.wait_ge(wts_ready, n - 2)
                    fn(gel[:, (n - 1) % 2, :], dots[:, (n - 1) % 2, :], ACT.Gelu).then_inc(gelu_done, 1)
                if m >= 0:
                    q = m // PK
                    act.wait_ge(wts_ready, q + 1)
                    if m >= NB:
                        act.wait_ge(v_used, m - NB + 1)
                    fn(diag[:, m % NB, :], ident, ACT.Copy, scale=wts[:, q % 2, k:k + 1]).then_inc(diag_ready, 1)
                for piece in behind.get(s, ()):
                    front_piece(*piece)

        @block.vector
        def _(dve):
            steps, newest = [0], []
            v = nc.vector

            def step(ins):
                steps[0] += 1
                return tell(ins, dve_step, steps[0])

            def tell(ins, s, value):
                ins.then_inc(s, 1)
                newest[:] = [(s, value)]
                return s, value

            def after(mark=None):
                dve.wait_ge(*(mark or newest[0]))
                return v

            def rsqrt(y, var, t, done=None):
                step(after().tensor_scalar(t.bitcast(U32), var.bitcast(U32), 1, None, ALU.logical_shift_right))
                step(after().tensor_scalar(y.bitcast(U32), t.bitcast(U32), -1.0, float(0x5F3759DF), ALU.mult, ALU.add))
                for n in range(3):
                    step(after().tensor_tensor(t, y, y, ALU.mult))
                    step(after().scalar_tensor_tensor(out=t, in0=t, scalar=-0.5, in1=var, op0=ALU.mult, op1=ALU.mult))
                    ins = after().scalar_tensor_tensor(out=y, in0=t, scalar=1.5, in1=y, op0=ALU.add, op1=ALU.mult)
                    if done and n == 2:
                        tell(ins, done, 1)
                    else:
                        step(ins)

            step(v.memset(ones[:, :], 1.0))
            dve.wait_ge(rowsT_ready, 1)
            tell(v.tensor_copy(cols[:, 0:NROWS], acc[1][:, 0:NROWS]), cols_ready, 1)
            dve.wait_ge(exp_c, 1)
            step(after().tensor_scalar(ecol, ecol, 1.0, None, ALU.add))
            step(after().reciprocal(ecol, ecol))
            tell(after().tensor_tensor(scol, ecol, cols[:, R_C:R_C + 8], ALU.mult), scol_ready, 1)

            dve.wait_ge(xss_ready, NT)
            step(v.tensor_scalar(var8[:, 0:NT], ssx, 1.0 / D, EPS, ALU.mult, ALU.add))
            rsqrt(y8[:, 0:NT], var8[:, 0:NT], t8[:, 0:NT], done=x_scale_ready)

            def ada_partial(a):
                w, marks = chunk_loaded(dve, "ada", a), [newest[0], newest[0]]
                if a >= 2:
                    dve.wait_ge(modcol_ready, a - 1)
                for k in range(KT):
                    for half in range(2):
                        cut = slice(256 * half, 256 * half + 256)
                        o = partial[:, a % 2, cut]
                        after(marks[half])
                        if k == 0:
                            ins = v.tensor_scalar(o, w[:, 0, cut], scol[:, 0:1], None, ALU.mult)
                        else:
                            ins = v.scalar_tensor_tensor(out=o, in0=w[:, k, cut], scalar=scol[:, k:k + 1], in1=o,
                                                         op0=ALU.mult, op1=ALU.add)
                        if (k, half) == (KT - 1, 1):
                            tell(ins, partial_ready[a % 2], a // 2 + 1)
                        else:
                            marks[half] = step(ins)

            dve.wait_ge(scol_ready, 1)
            step(v.memset(small[:, 96:97], 0.0))
            for a in range(4):
                ada_partial(a)
            dve.wait_ge(modcol_ready, 4)
            step(v.tensor_tensor(b1, modcol[:, 0:8], cols[:, R_ADAB:R_ADAB + 8], ALU.add))
            step(v.tensor_tensor(a1, modcol[:, 8:16], cols[:, R_ADAB + 8:R_ADAB + 16], ALU.add))
            step(after().scalar_tensor_tensor(out=a1, in0=a1, scalar=1.0, in1=cols[:, R_N1:R_N1 + 8], op0=ALU.add, op1=ALU.mult))
            after()
            dve.wait_ge(turn_taken, TURN_X)
            turns = TURN_X
            for k in range(KT):
                v.tensor_scalar(hT[:, k, :], hT[:, k, :], a1[:, k:k + 1], b1[:, k:k + 1], ALU.mult,
                                ALU.add).then_inc(hT_ready, 1)
            dve.wait_ge(pool_in, 48)
            tell(v.tensor_tensor(poolw, poolw, pscale, ALU.mult), poolw_ready, 1)

            staged = 0

            def take_turn(what, j):
                nonlocal turns, staged
                dve.wait_ge(turned, turns + 1)
                src = T[turns % 2]
                turns += 1
                if what == "k":
                    last = v.tensor_scalar(keysT[:, :, j * P:(j + 1) * P], src[:, :].rearrange("p (a n) -> p a n", a=4),
                                           cols[:, R_KG:R_KG + 1], None, ALU.mult)
                elif what == "keys":
                    last = v.tensor_copy(skT[:, 4 * j:4 * j + 4, :].rearrange("p a n -> p (a n)"), src[:, :])
                else:
                    e = staged
                    staged += 1
                    if e >= 3:
                        dve.wait_ge(spilled[e % 3], 16 * (e // 3))
                    if what == "q":
                        last = v.tensor_scalar(stage[:, e % 3, :], src[:, :], cols[:, R_QG:R_QG + 1], None, ALU.mult)
                    else:
                        last = v.tensor_copy(stage[:, e % 3, :], src[:, :])
                tell(last, turn_taken, turns)

            for i in range(ITEMS + 2):
                if i < ITEMS:
                    ch, j = item(i)
                    b = i % 2
                    n3 = normed[:, b, :].rearrange("p (h n) -> p h n", h=8)
                    if ch in ("q", "k"):
                        dve.wait_ge(item_squared, sum(1 for m in range(i + 1) if item(m)[0] in ("q", "k")))
                        step(after().reduce_sum(ss8, square[:, b, :].rearrange("p (h n) -> p h n", h=8), AX_X))
                        step(after().tensor_scalar(var8, ss8, 1.0 / HD, EPS, ALU.mult, ALU.add))
                        rsqrt(y8, var8, t8)
                        step(after().tensor_tensor(y8, y8, cst[:, C_HK:C_HK + 8] if ch == "q" else cst[:, C_HK + 8:C_HK + 16], ALU.mult))
                        dve.wait_ge(turned, turns)
                        tell(after().tensor_tensor(n3, A[b][:, :].rearrange("p (h n) -> p h n", h=8),
                                                   y8.unsqueeze(2).broadcast_to([P, 8, HD]), ALU.mult),
                             normed_ready[b], normed_count(i))
                if is_turned(i - 1):
                    take_turn(*item(i - 1))
                if (j := mix_at(i)) is not None:
                    dve.wait_ge(mixed_squared, j + 1)
                    step(after().tensor_scalar(var8[:, 0:1], sspool[:, j:j + 1], 1.0 / 512, EPS, ALU.mult, ALU.add))
                    rsqrt(y8[:, 0:1], var8[:, 0:1], t8[:, 0:1])
                    dve.wait_ge(turned, turns)
                    tell(after().tensor_scalar(pool_n, B[1][:, :], y8[:, 0:1], None, ALU.mult), mixed_taken, j + 1)
                if (j := poolturn_at(i)) is not None:
                    take_turn("pool", j)
                if keys_at(i) is not None:
                    take_turn("keys", keys_at(i))
                if i in DVE_ADA_AT:
                    ada_partial(DVE_ADA_AT[i])
                if i == MODS_AT:
                    dve.wait_ge(modcol_ready, 10)
                    ab = cols[:, R_ADAB:R_ADAB + 48]
                    v.tensor_tensor(b2, modcol[:, 24:32], ab[:, 24:32], ALU.add)
                    step(v.tensor_tensor(a2, modcol[:, 32:40], ab[:, 32:40], ALU.add))
                    tell(after().scalar_tensor_tensor(out=a2, in0=a2, scalar=1.0, in1=cols[:, R_N2:R_N2 + 8],
                                                      op0=ALU.add, op1=ALU.mult), mod_taken, 1)
                if i in ROW_AT:
                    r = ROW_AT[i]
                    row = (gate1[0], gate1[1], gate2[:, 0:512], gate2[:, 512:1024])[r]
                    dve.wait_ge(modcol_ready, GATES[r] + 1)
                    dve.wait_ge(gate_bias_in, 64)
                    tell(v.tensor_tensor(row, row, acc[0][:, :], ALU.add), row_taken, r + 1)

            def front_piece(j, i):
                W = keys_of(j)
                dist = cst[:, C_DIST + SEQ - W:C_DIST + SEQ]
                if i < TOP:
                    i -= 2
                    if j == 0 or i < 0:
                        return
                    n = 8 * (j - 1) + i
                    if i == 0:
                        dve.wait_ge(attT_ready, j)
                    else:
                        dve.wait_ge(relu_used, n)
                    dve.wait_ge(relu_done, n + 1)
                    w = widx[:, j, i:i + 1]
                    if i == 0:
                        ins = after().tensor_scalar(score[:, 0:W], pr[:, 0, 0:W], w, None, ALU.mult)
                    else:
                        ins = v.scalar_tensor_tensor(out=score[:, 0:W], in0=pr[:, i % 2, 0:W], scalar=w,
                                                     in1=score[:, 0:W], op0=ALU.mult, op1=ALU.add)
                    tell(ins, relu_used, n + 1)
                elif i < ATT:
                    if j == 0:
                        if i == TOP:
                            step(after().tensor_copy(bias[:, 0:W], dist))
                            step(after().memset(bias[0:HD, W - HD:W], MASKED))
                        return
                    if i == TOP:
                        step(after().memset(score[0:HD, W - HD:W], -MASKED))
                    if i < TOP + TOPK // 8:
                        step(after().max(m8, score[:, 0:W]))
                        step(after().match_replace(out=score[:, 0:W], in_to_replace=m8, in_values=score[:, 0:W],
                                                   imm_value=TAKEN))
                    else:
                        step(after().tensor_scalar(score[:, 0:W], score[:, 0:W], -2e38, MASKED, ALU.is_gt, ALU.mult))
                        step(after().tensor_tensor(bias[:, 0:W], score[:, 0:W], dist, ALU.add))
                elif i < END:
                    h = i - ATT - 1
                    if 0 <= h < HEADS:
                        n = 8 * j + h
                        dve.wait_ge(logits, n + 1)
                        if n >= 2:
                            dve.wait_ge(expd, n - 1 if h else 8 * j)
                        tell(after().tensor_tensor_reduce(
                            out=lg[:, h % 2, 0:W], in0=bias[:, 0:W], in1=A[h % 2][:, 0:W], scale=2.0 ** -(h + 1),
                            scalar=3e38, op0=ALU.add, op1=ALU.min, accum_out=mn8[:, h:h + 1]), biased, n + 1)
                elif i == END:
                    dve.wait_ge(pv_done, 8 * j + 8)
                    o3 = score[:, :].rearrange("p (h n) -> p h n", h=8)
                    sq = lg[:, 0, :]
                    step(after().reciprocal(rr8, rs8))
                    tell(after().tensor_tensor(o3, B[0][:, :].rearrange("p (h n) -> p h n", h=8),
                                               rr8.unsqueeze(2).broadcast_to([P, 8, HD]), ALU.mult), att_read, j + 1)
                    step(after().tensor_tensor(sq, score[:, :], score[:, :], ALU.mult))
                    step(after().reduce_sum(ss8, sq.rearrange("p (h n) -> p h n", h=8), AX_X))
                    step(after().tensor_scalar(var8, ss8, 1.0 / HD, EPS, ALU.mult, ALU.add))
                    rsqrt(y8, var8, t8)
                    tell(after().tensor_tensor(o3, o3, y8.unsqueeze(2).broadcast_to([P, 8, HD]), ALU.mult),
                         att_ready, j + 1)
                elif i == X2:
                    xt = xts[j % 2]
                    dve.wait_ge(xt_loaded[j % 2], 16 * (j // 2 + 1))
                    dve.wait_ge(out_proj, j + 1)
                    v.tensor_tensor(xt[:, 0:512], xt[:, 0:512], A[0][:, :], ALU.add)
                    tell(v.tensor_tensor(xt[:, 512:1024], xt[:, 512:1024], A[1][:, :], ALU.add), x2_ready, j + 1)
                elif i == XN2:
                    dve.wait_ge(x2_squared, j + 1)
                    step(after().tensor_scalar(var8[:, 0:1], ssx[:, 0:1], 1.0 / D, EPS, ALU.mult, ALU.add))
                    rsqrt(y8[:, 0:1], var8[:, 0:1], t8[:, 0:1])
                    if j >= 2:
                        dve.wait_ge(u_used, SLOTS * (j - 1))
                    tell(after().tensor_scalar(front[:, 1 + j % 2, :], xts[j % 2], y8[:, 0:1], None, ALU.mult),
                         xn2_ready, j + 1)
                elif i == H2_MOD:
                    for half in range(2):
                        dve.wait_ge(xn2T, 2 * j + half + 1)
                        for b in range(4):
                            k = 4 * half + b
                            last = v.tensor_scalar(h2T[:, k * P:(k + 1) * P], T[half][:, b * P:(b + 1) * P],
                                                   a2[:, k:k + 1], b2[:, k:k + 1], ALU.mult, ALU.add)
                        tell(last, h2T_ready, 2 * j + half + 1)
                elif i >= PEER + 5:
                    g, part = divmod(i - PEER - 5, 4)
                    if part in (0, 2, 3):
                        (top_of_blocks, None, top_sums, pick)[part](j, g)

            def top16(rows):
                marks = [newest[0]] * len(rows)

                def each(make):
                    for n, row in enumerate(rows):
                        after(marks[n])
                        marks[n] = step(make(*row))

                each(lambda val, at, src, w: v.max(val[:, 0:8], src))
                each(lambda val, at, src, w: v.match_replace(out=w, in_to_replace=val[:, 0:8], in_values=src,
                                                             imm_value=TAKEN))
                each(lambda val, at, src, w: v.max_index(at[:, 0:8], val[:, 0:8], src))
                each(lambda val, at, src, w: v.max(val[:, 8:16], w))
                each(lambda val, at, src, w: v.max_index(at[:, 8:16], val[:, 8:16], w))

            def top_of_blocks(j, g):
                dve.wait_ge(pscores, 4 * j + g + 1)
                top16([(topv[:, 16 * b:16 * b + 16], topi[:, 16 * b:16 * b + 16], A[g % 2][:, b * P:(b + 1) * P],
                        wk[:, b * P:(b + 1) * P]) for b in range(4)])
                tell(after().tensor_copy(topf[:, :], topi[:, :]), pscores_taken, 4 * j + g + 1)

            def top_sums(j, g):
                cand = lg[:, 0, :]
                for h in range(2):
                    f = topv[:, 32 * h:32 * h + 16].unsqueeze(2).broadcast_to([P, 16, 16])
                    s = topv[:, 32 * h + 16:32 * h + 32].unsqueeze(1).broadcast_to([P, 16, 16])
                    ins = v.tensor_tensor(cand[:, 256 * h:256 * h + 256].rearrange("p (a b) -> p a b", b=16), f, s, ALU.add)
                step(ins)
                at = 32 * g
                top16([(cval[:, at + 16 * h:at + 16 * h + 16], cpos[:, 16 * h:16 * h + 16],
                        cand[:, 256 * h:256 * h + 256], wk[:, 256 * h:256 * h + 256]) for h in range(2)])
                g3 = gates[:, j % 2, at:at + 32].rearrange("p (h k) -> p h k", h=2)
                c3 = cval[:, at:at + 32].rearrange("p (h k) -> p h k", h=2)
                tell(after().tensor_tensor(g3, c3, c3[:, :, 0:1].broadcast_to([P, 2, PK]), ALU.subtract),
                     gate_in, 4 * j + g + 1)

            def pick(j, g):
                ones2 = [a.rearrange("p (a b) -> p a b", b=16) for a in (lg[:, 1, :], wk[:, :])]
                iota = cst[:, C_IOTA:C_IOTA + 16].unsqueeze(1).broadcast_to([P, 32, 16])
                marks = [step(after().tensor_scalar(cpart[:, 0, :], cpos[:, :], 4, None, ALU.logical_shift_right)),
                         step(v.tensor_scalar(cpart[:, 1, :], cpos[:, :], 15, None, ALU.bitwise_and))]
                for side in range(2):
                    marks[side] = step(after(marks[side]).tensor_tensor(
                        ones2[side], cpart[:, side, :].unsqueeze(2).broadcast_to([P, 32, 16]), iota, ALU.is_equal))
                for side in range(2):
                    after(marks[side])
                    for h in range(2):
                        key = topf[:, 32 * h + 16 * side:32 * h + 16 * side + 16].unsqueeze(1).broadcast_to([P, 16, 16])
                        one = ones2[side][:, 16 * h:16 * h + 16, :]
                        ins = v.tensor_tensor(one, one, key, ALU.mult)
                    marks[side] = step(ins)
                for side in range(2):
                    step(after(marks[side]).reduce_sum(csel[:, side, :], ones2[side], AX_X))
                g3 = gates[:, j % 2, 32 * g:32 * g + 32].rearrange("p (h k) -> p h k", h=2)
                dve.wait_ge(gate_exp, 4 * j + g + 1)
                step(after().reduce_sum(gsum[:, 0:2], g3, AX_X))
                step(after().reciprocal(grec[:, 0:2], gsum[:, 0:2]))
                step(after().tensor_tensor(g3, g3, grec[:, 0:2].unsqueeze(2).broadcast_to([P, 2, PK]), ALU.mult))
                dve.wait_ge(h2_ready, 2 * j + 2)
                tell(after().scalar_tensor_tensor(out=eid[:, j % 2, 32 * g:32 * g + 32], in0=csel[:, 0, :], scalar=128.0,
                                                  in1=csel[:, 1, :], op0=ALU.mult, op1=ALU.add),
                     experts_ready, 4 * j + g + 1)

            for i in range(SPLIT):
                front_piece(0, i)
            for s in range(NT * SLOTS + PK + 1):
                n, k = divmod(s, PK)
                if s < NT * SLOTS:
                    j = s // SLOTS
                    dve.wait_ge(u_landed[s % NB], 16 * (s // NB + 1))
                    if k == 0 and n >= 2:
                        dve.wait_ge(gelu_done, n - 1)
                    buf = ubuf[s % NB]
                    v.scalar_tensor_tensor(out=buf, in0=buf, scalar=1.0, in1=front[:, 1 + j % 2, :], op0=ALU.mult,
                                           op1=ALU.mult, accum_out=dots[:, n % 2, k:k + 1]).then_inc(u_used, 1)
                if k == 0 and 1 <= n <= NT * PH:
                    m = n - 1
                    dve.wait_ge(gelu_done, m + 1)
                    if m >= 2:
                        dve.wait_ge(diag_ready, PK * (m - 1))
                    h = m % PH
                    v.tensor_tensor(wts[:, m % 2, :], gel[:, m % 2, :], gates[:, (m // PH) % 2, h * PK:(h + 1) * PK],
                                    ALU.mult).then_inc(wts_ready, 1)
                r = s - PK
                if r >= SLOTS and r % SLOTS == 0:
                    j = r // SLOTS - 1
                    dve.wait_ge(v_used, SLOTS * (j + 1))
                    x2 = xts[j % 2]
                    for half in range(2):
                        cut = slice(half * 512, (half + 1) * 512)
                        step(v.tensor_tensor(acc[half][:, :], acc[half][:, :], gate2[:, cut], ALU.mult))
                        ins = after().tensor_tensor(x2[:, cut], x2[:, cut], acc[half][:, :], ALU.add)
                        if half == 0:
                            step(ins)
                        else:
                            tell(ins, fin_ready, j + 1)
                for piece in behind.get(s, ()):
                    front_piece(*piece)


_INS = ["x", "c", "ada_w", "ada_b", "norm1_g", "w_in", "pool_w", "pool_scale", "pool_out_g", "q_norm_g",
        "k_norm_g", "attn_out_g", "w_out", "norm2_g", "peer_wq", "peer_subkeys", "peer_u", "peer_v"]


def kernel(**inputs):
    import numpy as _np
    import concourse.bacc as _bacc
    from concourse import mybir as _mybir
    from concourse.bass_utils import run_bass_kernel_spmd as _run

    nc = _bacc.Bacc("TRN2", target_bir_lowering=False, num_devices=1, dynamic_dma_scratch_size=8192)
    arrays, args = {}, []
    for name in _INS + ["const"]:
        a = constants() if name == "const" else _np.ascontiguousarray(inputs[name])
        arrays[f"in_{name}"] = a
        args.append(nc.dram_tensor(f"in_{name}", a.shape, _mybir.dt.from_np(a.dtype), kind="ExternalInput").ap())
    out = nc.dram_tensor("out_0", (1, SEQ, D), F32, kind="ExternalOutput").ap()
    hymba_block(nc, *args, out)
    r = _run(nc, [arrays], core_ids=[0])
    return r.results[0]["out_0"]
```
